# Optimizing a Trainium2 kernel written in Bass

```python
import math
import jax, jax.numpy as jnp
from jax import lax
import numpy as np

D_MODEL = 1024
BATCH = 1
SEQ = 1024
DEPTH = 1
DEC_BATCH = 8
DEC_SEQ = 8
PAST_LEN = 8192
PAGE_SIZE = 128

GLA_WIDTH = D_MODEL // 2
CONV_WIDTH = D_MODEL - GLA_WIDTH
GLA_HEADS = 4
GLA_DV = GLA_WIDTH // GLA_HEADS
GLA_DK = GLA_DV // 2
GLA_LOWRANK = 16
GLA_TAU = 16.0
GLA_CHUNK = 64
CONV_K = 31
PLE_DIM = 256
N_GROUPS = 4
EXPERTS_PER_GROUP = 8
EXPERT_FF = 256
TOP_K = 2
EPS = 1e-6

Q_COLS = GLA_HEADS * GLA_DK
V_COLS = GLA_HEADS * GLA_DV
SPLITS = (Q_COLS, 2 * Q_COLS, 2 * Q_COLS + V_COLS, 2 * Q_COLS + 2 * V_COLS,
          2 * Q_COLS + 2 * V_COLS + GLA_LOWRANK)
IN_COLS = 2 * Q_COLS + 2 * V_COLS + GLA_LOWRANK + 2 * CONV_WIDTH

kernel_name = "hymba_gla_conformer_hmoe_step"

def rmsnorm(x, g):
    xf = x.astype(jnp.float32)
    y = xf * lax.rsqrt(jnp.mean(xf * xf, axis=-1, keepdims=True) + EPS)
    return (y * g.astype(jnp.float32)).astype(x.dtype)

def layernorm(x, g, b):
    xf = x.astype(jnp.float32)
    mu = jnp.mean(xf, axis=-1, keepdims=True)
    xc = xf - mu
    y = xc * lax.rsqrt(jnp.mean(xc * xc, axis=-1, keepdims=True) + EPS)
    return (y * g.astype(jnp.float32) + b.astype(jnp.float32)).astype(x.dtype)

def gla_chunked(q, k, v, log_a, s0):
    B, T, H, _ = q.shape
    C = math.gcd(T, GLA_CHUNK)
    n = T // C

    def to_chunks(a):
        return jnp.moveaxis(a.astype(jnp.float32).reshape(B, n, C, H, a.shape[-1]), 1, 0)

    causal = jnp.tril(jnp.ones((C, C), dtype=bool))[None, :, :, None, None]

    def step(S, blk):
        qb, kb, vb, ab = blk
        b = jnp.cumsum(ab, axis=1)
        decay = jnp.exp(jnp.where(causal, b[:, :, None] - b[:, None, :], -jnp.inf))
        scores = jnp.sum(qb[:, :, None] * decay * kb[:, None], axis=-1)
        o_intra = jnp.einsum('btsh,bshv->bthv', scores, vb)
        o_inter = jnp.einsum('bthk,bhkv->bthv', qb * jnp.exp(b), S)
        b_last = b[:, -1]
        S_new = jnp.exp(b_last)[..., None] * S + jnp.einsum(
            'bshk,bshv->bhkv', kb * jnp.exp(b_last[:, None] - b), vb)
        return S_new, o_intra + o_inter

    S, o = lax.scan(step, s0.astype(jnp.float32),
                    (to_chunks(q), to_chunks(k), to_chunks(v), to_chunks(log_a)))
    return jnp.moveaxis(o, 0, 1).reshape(B, T, H, -1), S

def causal_depthwise_conv(u, buf, w, b):
    full = jnp.concatenate([buf.astype(u.dtype), u], axis=1)
    y = lax.conv_general_dilated(full, w[:, None, :].astype(u.dtype), window_strides=(1,),
                                 padding='VALID', dimension_numbers=('NWC', 'WIO', 'NWC'),
                                 feature_group_count=u.shape[-1])
    return y + b, full[:, -(CONV_K - 1):]

def hier_moe(x, w_grp, b_grp, w_er, b_er, w_gate, w_up, w_down):
    N = x.shape[0]
    xf = x.astype(jnp.float32)
    grp_logits = xf @ w_grp.astype(jnp.float32) + b_grp.astype(jnp.float32)
    grp_probs = jax.nn.softmax(grp_logits, axis=-1)
    g_sel = jnp.argmax(grp_logits, axis=-1)
    g_w = jnp.take_along_axis(grp_probs, g_sel[:, None], axis=-1)
    exp_logits = jnp.einsum('nd,gde->nge', xf, w_er.astype(jnp.float32)) + b_er.astype(jnp.float32)
    sel_logits = jnp.take_along_axis(exp_logits, g_sel[:, None, None], axis=1)[:, 0]
    top_v, top_i = lax.top_k(sel_logits, TOP_K)
    top_w = jax.nn.softmax(top_v, axis=-1) * g_w
    within = jnp.sum(jax.nn.one_hot(top_i, EXPERTS_PER_GROUP) * top_w[..., None], axis=1)
    combine = (jax.nn.one_hot(g_sel, N_GROUPS)[:, :, None] * within[:, None, :]).astype(x.dtype)
    y = jnp.zeros_like(x)
    for gi in range(N_GROUPS):
        hg = jax.nn.silu(jnp.einsum('nd,edf->nef', x, w_gate[gi])) * jnp.einsum('nd,edf->nef', x, w_up[gi])
        y = y + jnp.einsum('nef,efd->nd', hg * combine[:, gi, :, None], w_down[gi])
    return y

def layer(h, p_l, s0, buf0, g_mix, w_in, w_forget_up, b_forget, g_gla_out, w_conv, b_conv,
          g_conv_ln, b_conv_ln, w_out, g_ffn, w_grp_router, b_grp_router, w_exp_router,
          b_exp_router, w_exp_gate, w_exp_up, w_exp_down, g_ple, w_ple_gate, w_ple_proj):
    B, T, _ = h.shape
    xn = rmsnorm(h, g_mix)
    z = xn @ w_in
    q, k, v, og, lr, cv = jnp.split(z, SPLITS, axis=-1)
    q = q.reshape(B, T, GLA_HEADS, GLA_DK) * (GLA_DK ** -0.5)
    k = k.reshape(B, T, GLA_HEADS, GLA_DK)
    v = v.reshape(B, T, GLA_HEADS, GLA_DV)
    log_a = jax.nn.log_sigmoid((lr @ w_forget_up + b_forget).astype(jnp.float32)) / GLA_TAU
    o, s_new = gla_chunked(q, k, v, log_a.reshape(B, T, GLA_HEADS, GLA_DK), s0)
    o = rmsnorm(o.astype(h.dtype), g_gla_out) * jax.nn.silu(og.reshape(B, T, GLA_HEADS, GLA_DV))
    o = o.reshape(B, T, GLA_WIDTH)
    a, gate = jnp.split(cv, 2, axis=-1)
    u = a * jax.nn.sigmoid(gate)
    c, buf_new = causal_depthwise_conv(u, buf0, w_conv, b_conv)
    c = jax.nn.silu(layernorm(c, g_conv_ln, b_conv_ln))
    h = h + jnp.concatenate([o, c], axis=-1) @ w_out
    xn = rmsnorm(h, g_ffn).reshape(B * T, D_MODEL)
    h = h + hier_moe(xn, w_grp_router, b_grp_router, w_exp_router, b_exp_router,
                     w_exp_gate, w_exp_up, w_exp_down).reshape(B, T, D_MODEL)
    xn = rmsnorm(h, g_ple)
    h = h + jax.nn.sigmoid(xn @ w_ple_gate) * (p_l @ w_ple_proj)
    return h, s_new, buf_new

def trunk(x, p, s_init, buf_init, layer_weights, g_final):
    h = x
    states, bufs = [], []
    for l in range(DEPTH):
        h, s, buf = layer(h, p[l], s_init[l], buf_init[l], *(w[l] for w in layer_weights))
        states.append(s)
        bufs.append(buf)
    return rmsnorm(h, g_final), jnp.stack(states), jnp.stack(bufs)

def setup_inputs(seed: int = 0) -> dict:
    key = jax.random.key(seed)
    ks = iter(jax.random.split(key, 40))

    def nrm(shape, scale=1.0):
        return jax.random.normal(next(ks), shape, jnp.float32) * scale

    def gain(shape):
        return 1.0 + nrm(shape, 0.01)

    G, E, F, D = N_GROUPS, EXPERTS_PER_GROUP, EXPERT_FF, D_MODEL
    return {
        "x_prompt": nrm((BATCH, SEQ, D)),
        "x_sample": nrm((DEC_BATCH, DEC_SEQ, D)),
        "state_gla": nrm((DEPTH, DEC_BATCH, GLA_HEADS, GLA_DK, GLA_DV)),
        "state_conv": nrm((DEPTH, DEC_BATCH, CONV_K - 1, CONV_WIDTH), 0.5),
        "p_prompt": nrm((DEPTH, BATCH, SEQ, PLE_DIM)),
        "p_sample": nrm((DEPTH, DEC_BATCH, DEC_SEQ, PLE_DIM)),
        "g_mix": gain((DEPTH, D)),
        "w_in": nrm((DEPTH, D, IN_COLS), D ** -0.5),
        "w_forget_up": nrm((DEPTH, GLA_LOWRANK, Q_COLS), GLA_LOWRANK ** -0.5),
        "b_forget": nrm((DEPTH, Q_COLS), 0.1),
        "g_gla_out": gain((DEPTH, GLA_DV)),
        "w_conv": nrm((DEPTH, CONV_K, CONV_WIDTH), CONV_K ** -0.5),
        "b_conv": nrm((DEPTH, CONV_WIDTH), 0.01),
        "g_conv_ln": gain((DEPTH, CONV_WIDTH)),
        "b_conv_ln": nrm((DEPTH, CONV_WIDTH), 0.01),
        "w_out": nrm((DEPTH, D, D), D ** -0.5),
        "g_ffn": gain((DEPTH, D)),
        "w_grp_router": nrm((DEPTH, D, G), D ** -0.5),
        "b_grp_router": nrm((DEPTH, G), 0.01),
        "w_exp_router": nrm((DEPTH, G, D, E), D ** -0.5),
        "b_exp_router": nrm((DEPTH, G, E), 0.01),
        "w_exp_gate": nrm((DEPTH, G, E, D, F), D ** -0.5),
        "w_exp_up": nrm((DEPTH, G, E, D, F), D ** -0.5),
        "w_exp_down": nrm((DEPTH, G, E, F, D), F ** -0.5),
        "g_ple": gain((DEPTH, D)),
        "w_ple_gate": nrm((DEPTH, D, D), D ** -0.5),
        "w_ple_proj": nrm((DEPTH, PLE_DIM, D), PLE_DIM ** -0.5),
        "g_final": gain((D,)),
    }

def reference(x_prompt, x_sample, state_gla, state_conv, p_prompt, p_sample, g_mix, w_in,
              w_forget_up, b_forget, g_gla_out, w_conv, b_conv, g_conv_ln, b_conv_ln, w_out,
              g_ffn, w_grp_router, b_grp_router, w_exp_router, b_exp_router, w_exp_gate,
              w_exp_up, w_exp_down, g_ple, w_ple_gate, w_ple_proj, g_final):
    layer_weights = (g_mix, w_in, w_forget_up, b_forget, g_gla_out, w_conv, b_conv, g_conv_ln,
                     b_conv_ln, w_out, g_ffn, w_grp_router, b_grp_router, w_exp_router,
                     b_exp_router, w_exp_gate, w_exp_up, w_exp_down, g_ple, w_ple_gate, w_ple_proj)
    n_prompt = x_prompt.shape[0]
    s_zero = jnp.zeros((DEPTH, n_prompt, GLA_HEADS, GLA_DK, GLA_DV), jnp.float32)
    buf_zero = jnp.zeros((DEPTH, n_prompt, CONV_K - 1, CONV_WIDTH), x_prompt.dtype)
    y_prompt, sg_prompt, sc_prompt = trunk(x_prompt, p_prompt, s_zero, buf_zero, layer_weights, g_final)
    y_sample, sg_sample, sc_sample = trunk(x_sample, p_sample, state_gla, state_conv, layer_weights, g_final)
    return (y_prompt, y_sample, sg_prompt, sg_sample, sc_prompt, sc_sample)


_drawn_inputs = setup_inputs


def setup_inputs(seed=0):
    import zlib

    import numpy as np

    out = dict(_drawn_inputs(seed))
    spreads = {}
    factors = {'g_gla_out': 3.573,
     'b_conv': 3.93,
     'g_conv_ln': 5.035,
     'b_conv_ln': 8.0,
     'g_ffn': 3.343,
     'b_exp_router': 3.847,
     'g_ple': 64.0,
     'g_final': 38.584,
     'b_grp_router': 8.0}
    for name, (base, spread) in spreads.items():
        noise = np.random.default_rng([zlib.crc32(name.encode()), seed]).standard_normal(out[name].shape)
        drawn = base * np.exp(spread * noise) if base else spread * noise
        out[name] = __import__('jax').numpy.asarray(drawn.astype(out[name].dtype))
    for name, factor in factors.items():
        out[name] = (out[name] * factor).astype(out[name].dtype)
    return out
```

```python
from contextlib import ExitStack

import concourse.bass as bass
import numpy as np
from concourse import mybir
from concourse.alu_op_type import AluOpType as ALU

F32 = mybir.dt.float32
I32 = mybir.dt.int32
ACT = mybir.ActivationFunctionType
AX = mybir.AxisListType.X

P = 128
D = 1024
KC = D // P
SEQ = 1024
NB, TB = 8, 8
NS = NB * TB
NT = SEQ // P + 1
TOK = NT * P
H, DK, DV = 4, 64, 128
QW, VW = H * DK, H * DV
LR = 16
TW = 2 * QW + 2 * VW + LR
CW = 512
CC = CW // P
K = 31
HIST = K - 1
BLK = 384
NBLK = TOK // BLK
G, E, FF = 4, 8, 256
NE = G * E
FC = FF // P
PLE = 256
PC = PLE // P
EPS = 1e-6
TAU = 16.0
MID = P // 2
BIG = 1e30
EXTRA = (2 * (SEQ + NS)) // (P + 1)
NTILE = NE + EXTRA

CONSTS = [("ident", P), ("tric", P), ("tris", P), ("cmask", P), ("cmasks", P), ("upper", P), ("ones", P),
          ("halves", 2), ("seqsum", NB), ("seqone", NB), ("desc8", E), ("desc4", G), ("eidx", NE),
          ("steps", E), ("tidx", EXTRA), ("count", P), ("token", NT)]
CAT, _at = {}, 0
for _name, _w in CONSTS:
    CAT[_name] = (_at, _w)
    _at += _w
CONST_W = _at


def constants():
    s, t = np.arange(P)[:, None], np.arange(P)[None, :]
    c = np.zeros((P, CONST_W), np.float32)

    def put(name, v):
        a, w = CAT[name]
        c[:, a:a + w] = v

    same = (s // TB == t // TB)
    put("ident", s == t)
    put("tric", ((s <= t) * 1.0 - (s < MID) * 1.0) / TAU)
    put("tris", (same & (s <= t)) / TAU)
    put("cmask", s <= t)
    put("cmasks", same & (s <= t))
    put("upper", s < t)
    put("ones", 1.0)
    put("halves", np.concatenate([s < MID, s >= MID], 1) / TAU)
    b = np.arange(NB)[None, :]
    put("seqsum", (s // TB == b) / TAU)
    put("seqone", s // TB == b)
    put("desc8", E - np.arange(E)[None, :])
    put("desc4", G - np.arange(G)[None, :])
    put("eidx", np.arange(NE)[None, :])
    put("steps", P * (1 + np.arange(E))[None, :])
    put("tidx", np.arange(EXTRA)[None, :])
    put("count", t)
    token = np.arange(NT)[None, :] * P + s
    put("token", token * (token < SEQ + NS))
    return c


def experts(eng, body):
    for t in range(4):
        body(t, t % 3)
    with eng.Fori(1, (NE - 2) // 3) as i:
        for k in range(1, 4):
            body(3 * i + k, k % 3)
    body(NE - 1, (NE - 1) % 3)


def extra(eng, count, body):
    with eng.Fori(0, EXTRA // 2) as i:
        for j in range(2):
            with eng.If(count > 2 * i + j):
                body(2 * i + j, 2 - j)


def embeds(eng, body):
    body(0, 0)
    body(1, 1)
    with eng.Fori(1, (NT - 3) // 2) as i:
        body(2 * i, 0)
        body(2 * i + 1, 1)
    for n in range(NT - 3, NT):
        body(n, n % 2)


def turn_of(t, s):
    return t // 3 if isinstance(t, int) else (t - s) // 3


def extra_turn(t, s):
    return 16 * ((NE + 2 - s) // 3) + 8 * (t - (2 - s)) + 16


def hold(eng, passed):
    eng.sem_inc(passed, 1)


def late(n, k):
    return not isinstance(n, int) or n >= k


def tiles(eng, body):
    body(0, 0)
    body(1, 1)
    with eng.Fori(1, (NT - 1) // 2) as i:
        body(2 * i, 0)
        body(2 * i + 1, 1)
    body(NT - 1, 0)


def bass_decoder_step(nc, a, o):
    with ExitStack() as ctx:
        arena = ctx.enter_context(nc.sbuf_tensor("arena", [P, 40888], F32))
        psum = ctx.enter_context(nc.psum_tensor("psum", [P, 8, 512], F32))

        def at(start, *shape):
            n = int(np.prod(shape))
            v = arena[:, start:start + n]
            if len(shape) == 2:
                v = v.rearrange("p (a b) -> p a b", b=shape[1])
            elif len(shape) == 3:
                v = v.rearrange("p (a b c) -> p a b c", b=shape[1], c=shape[2])
            return v

        def sb(name, *shape, dt=F32, parts=P):
            return ctx.enter_context(nc.sbuf_tensor(name, [parts, *shape], dt))

        def sem(name):
            return ctx.enter_context(nc.semaphore(name))

        R1, R2, R3, R4, R5 = 0, 9216, 21632, 30848, 36280
        xnT = at(R1, KC, TOK)
        wtok = at(R2, KC, TW)
        wcv = [at(R3 + 2048 * j, KC, 2 * P) for j in range(2)]
        a_sb = at(R3 + 4096, TOK)
        sg_sb = at(R3 + 4096 + TOK, TOK)
        xt = at(R2, NT, D)
        sqj = [at(R5 + 1024 * j, D) for j in range(2)]
        xs = [at(R5 + 2048 + 1024 * j, D) for j in range(2)]
        UW = HIST + SEQ
        SW = HIST + TB
        u = at(R4, CC, UW)
        us = at(R4 + CC * UW, CC, NB * SW).rearrange("p c (b t) -> p c b t", t=SW)
        cT = at(R5, CC, TOK)
        oraw = at(R3, NT, VW)
        gog = at(R3 + NT * VW, NT, VW)
        s0 = at(R2, NB, H * DV)[0:DK].rearrange("p b (h d) -> p b h d", d=DV)
        qm = at(R2 + 4096, H, NB, NS)[0:DK]
        km = at(R2 + 6144, NB, QW)
        csq = at(R4, CC, TOK)
        h = at(R2, NT, D)
        mean = at(R2 + NT * D, TOK)
        rstdb = at(R2 + NT * D + TOK, TOK)
        wout = at(R1, KC, D)
        catT = [at(R4 + 1024 * j, KC, P) for j in range(2)]
        xn2T = [at(R4 + 2048 + 1024 * j, KC, P) for j in range(2)]
        xn2 = [at(R2 + NT * D + 1024 * j, D) for j in range(2)]

        RT = R2 + NT * D
        M12 = at(RT, 2, NT, NE)
        Msum = at(RT + 576, NT, NE)
        rank = at(RT + 864, NT, NE)
        before = at(RT + 1152, NT + 1, NE)
        prod = at(RT + 1472, 2 * NT, NE)
        cmpe = at(RT + 2048, NE, E)
        cmpt = at(RT + 2304, EXTRA, NE)
        RS = R1 + KC * D
        gd = at(RS, NT, G)
        gsc = at(RS + 36, NT, G)
        ohg = at(RS + 72, NT, G)
        sel = at(RS + 108, NT, E)
        esc = at(RS + 180, NT, E)
        oh = [at(RS + 252 + 72 * m, NT, E) for m in range(2)]
        cmpr = at(RS + 396, 2 * NT, E)
        one = {n: at(RS + 540 + 9 * i, NT) for i, n in enumerate(["gmax", "gm", "gsum", "gw", "v1", "m1", "v2", "m2", "dv", "ev"])}
        two = {n: at(RS + 640 + 18 * i, 2 * NT) for i, n in enumerate(["rank", "exp", "ovb", "q", "isq", "t", "r", "fy"])}
        nx = at(RS + 810, NE)
        inc = at(RS + 842, NE)
        ovb = at(RS + 874, NE)
        et = at(RS + 906, EXTRA)
        ohr = at(R3 + 6144, 2 * NT, P)
        oht = at(R4 + 6144, 2 * NT, NTILE)
        WAT = [R1, R3, R4]
        wgu = [at(w, KC, 2 * FF) for w in WAT]
        wdn = [at(w + KC * 2 * FF, FC, D) for w in WAT]
        xg = [at(RT + D * s, D) for s in range(3)]
        xgT = [at(R3 + 6144 + D * s, KC, P) for s in range(3)]
        yt = [at(R1 + 6144 + D * s, D) for s in range(3)]
        sil = [at(R4 + 6144 + FF * s, FF) for s in range(3)]
        hg = at(R4 + 6912, FF)
        hT = at(R4 + 7168, FC, P)
        wple = [at(R1 + D * k, D) if k < 6 else at(R4 + 7992 + D * (k - 6), D) for k in range(KC)]
        yg = [[at(R3 + 2048 * j + D * m, D) for m in range(2)] for j in range(2)]
        xn3 = [at(R3 + 4096 + D * j, D) for j in range(2)]
        x3T = [at(R3 + 6144 + D * j, KC, P) for j in range(2)]
        yo = [at(RT + D * j, D) for j in range(2)]
        wproj = at(R4, PC, D)
        pT = [at(R4 + 2048 + 256 * j, PC, P) for j in range(2)]
        mixd = [at(R4 + 2560 + D * j, D) for j in range(2)]
        gfin = at(R4 + 4608, D)

        cst = sb("cst", CONST_W)
        C = {n: cst[:, s:s + w] for n, (s, w) in CAT.items()}
        xTs = [sb(f"xTs{j}", KC, P) for j in range(2)]
        g1 = sb("g1", D)
        ssq = sb("ssq", 2)
        std = sb("std", 2)
        rst = sb("rst", 2)
        wc = sb("wc", CC, K)
        cvec = sb("cvec", 3, CC)
        ggo = sb("ggo", 1)
        gghalf = sb("gghalf", 1)
        wf = sb("wf", QW, parts=LR + 1)
        lr_sb = sb("lr_sb", LR)
        lrT = sb("lrT", P, parts=LR + 1)
        absx = sb("absx", QW)
        la = sb("la", QW)
        E1 = sb("E1", QW)
        E2 = sb("E2", QW)
        EL = [sb(f"EL{j}", H, 2, parts=DK) for j in range(2)]
        ELs = sb("ELs", H, NB, parts=DK)
        v_sb = [sb(f"v{j}", VW) for j in range(2)]
        th = sb("th", VW)
        qk = sb("qk", 2 * QW)
        qkT = sb("qkT", 2 * H, P, parts=DK)
        PT = sb("PT", H, P)
        St = sb("St", H, DV, parts=DK)
        Smid = sb("Smid", H, DV, parts=DK)
        Slast = sb("Slast", H, DV, parts=DK)
        eps = sb("eps", 1)
        osq = sb("osq", 2, H)
        ostd = sb("ostd", 2, H)
        orst = sb("orst", 2, H)
        og = v_sb
        wr = sb("wr", KC, G + NE)
        brb = sb("brb", G + NE)
        logits = sb("logits", NT, G + NE)
        ids = sb("ids", NTILE, dt=I32)
        idx = [sb(f"idx{s}", 1, dt=I32) for s in range(3)]
        idy = [[sb(f"idy{j}{m}", 1, dt=I32) for m in range(2)] for j in range(2)]
        posY = sb("posY", 2 * NT, dt=I32)
        w12 = sb("w12", 2, NT)
        plan = sb("plan", EXTRA + 3, dt=I32)

        c_in = sem("c_in")
        g1_in = sem("g1_in")
        x_in = [sem(f"x_in{j}") for j in range(2)]
        ssq_rdy = sem("ssq_rdy")
        std_rdy = sem("std_rdy")
        rst_rdy = sem("rst_rdy")
        xs_rdy = sem("xs_rdy")
        xT_ps = sem("xT_ps")
        xnT_a = sem("xnT_a")
        xnT_v = sem("xnT_v")
        wcv_in = [sem(f"wcv_in{j}") for j in range(2)]
        cv_ps = sem("cv_ps")
        cv_sb = sem("cv_sb")
        u_rdy = sem("u_rdy")
        zero = sem("zero")
        conv = sem("conv")
        hist_in = sem("hist_in")
        cst_out = sem("cst_out")
        wtok_in = sem("wtok_in")
        xTs_rdy = sem("xTs_rdy")
        lr_ps = sem("lr_ps")
        lr_rdy = sem("lr_rdy")
        lrT_ps = sem("lrT_ps")
        lrT_rdy = sem("lrT_rdy")
        lap_ps = sem("lap_ps")
        absx_rdy = sem("absx_rdy")
        la_rdy = sem("la_rdy")
        b_ps = sem("b_ps")
        E_rdy = sem("E_rdy")
        qk_ps = sem("qk_ps")
        v_ps = sem("v_ps")
        og_ps = sem("og_ps")
        v_rdy = sem("v_rdy")
        th_rdy = sem("th_rdy")
        gog_rdy = sem("gog_rdy")
        qk_rdy = sem("qk_rdy")
        qkT_ps = sem("qkT_ps")
        qT_rdy = sem("qT_rdy")
        kT_rdy = sem("kT_rdy")
        sc_ps = sem("sc_ps")
        PT_rdy = sem("PT_rdy")
        o_ps = sem("o_ps")
        o_rdy = sem("o_rdy")
        U_ps = sem("U_ps")
        S_rdy = sem("S_rdy")
        Sm_rdy = sem("Sm_rdy")
        s0_in = sem("s0_in")
        smp = sem("smp")
        SU_ps = sem("SU_ps")
        SU_add = sem("SU_add")
        SU_out = sem("SU_out")
        csq_rdy = sem("csq_rdy")
        st_ps = sem("st_ps")
        ln_v = sem("ln_v")
        ln_std = sem("ln_std")
        ln_x = sem("ln_x")
        cT_rdy = sem("cT_rdy")
        wout_in = sem("wout_in")
        g2_in = sem("g2_in")
        osq_rdy = sem("osq_rdy")
        ostd_rdy = sem("ostd_rdy")
        orst_rdy = sem("orst_rdy")
        og_rdy = sem("og_rdy")
        oT_ps = sem("oT_ps")
        catT_o = sem("catT_o")
        catT_c = sem("catT_c")
        w_ps = sem("w_ps")
        x2_in = [sem(f"x2_in{j}") for j in range(2)]
        h_rdy = sem("h_rdy")
        ssq2_rdy = sem("ssq2_rdy")
        std2_rdy = sem("std2_rdy")
        rst2_rdy = sem("rst2_rdy")
        xn2_rdy = sem("xn2_rdy")
        xn2_out = [sem(f"xn2_out{j}") for j in range(2)]
        xn2T_ps = sem("xn2T_ps")
        xn2T_a = sem("xn2T_a")
        xn2T_v = sem("xn2T_v")
        lg_ps = sem("lg_ps")
        lg_rdy = sem("lg_rdy")
        out_st = sem("out_st")
        rt = sem("rt")
        ge_rdy = sem("ge_rdy")
        gd_rdy = sem("gd_rdy")
        ev_rdy = sem("ev_rdy")
        dv_rdy = sem("dv_rdy")
        M_rdy = sem("M_rdy")
        rk_ps = sem("rk_ps")
        pos_rdy = sem("pos_rdy")
        oh_rdy = sem("oh_rdy")
        ids_ps = sem("ids_ps")
        ids_rdy = sem("ids_rdy")
        idx_rdy = sem("idx_rdy")
        passed = sem("passed")
        passed_sp = sem("passed_sp")
        xg_in = [sem(f"xg_in{s}") for s in range(3)]
        gu_in = [sem(f"gu_in{s}") for s in range(3)]
        dn_in = [sem(f"dn_in{s}") for s in range(3)]
        xgT_ps = sem("xgT_ps")
        xgT_a = sem("xgT_a")
        xgT_v = sem("xgT_v")
        gu_ps = sem("gu_ps")
        sil_rdy = sem("sil_rdy")
        hg_rdy = sem("hg_rdy")
        hT_ps = sem("hT_ps")
        hT_rdy = sem("hT_rdy")
        y_ps = sem("y_ps")
        y_a = sem("y_a")
        y_v = sem("y_v")
        y_out = [sem(f"y_out{s}") for s in range(3)]
        y_all = sem("y_all")
        y_zero = sem("y_zero")
        moe_done = sem("moe_done")
        idy_rdy = sem("idy_rdy")
        yg_in = [[sem(f"yg_in{j}{m}") for m in range(2)] for j in range(2)]
        wple_in = sem("wple_in")
        pw_in = sem("pw_in")
        pT_in = [sem(f"pT_in{j}") for j in range(2)]
        add_rdy = sem("add_rdy")
        ssq3_rdy = sem("ssq3_rdy")
        std3_rdy = sem("std3_rdy")
        rst3_rdy = sem("rst3_rdy")
        xn3_rdy = sem("xn3_rdy")
        x3T_ps = sem("x3T_ps")
        x3T_a = sem("x3T_a")
        x3T_v = sem("x3T_v")
        pr_ps = sem("pr_ps")
        gt_ps = sem("gt_ps")
        sg_rdy = sem("sg_rdy")
        mix_rdy = sem("mix_rdy")
        ssq4_rdy = sem("ssq4_rdy")
        std4_rdy = sem("std4_rdy")
        rst4_rdy = sem("rst4_rdy")
        y_rdy = sem("y_rdy")
        fin_out = [sem(f"fin_out{j}") for j in range(2)]

        SMALL = [(wc[:], "w_conv"), (cvec[:], "conv_vecs"), (ggo[:], "g_gla_out"), (wf[:], "w_forget"),
                 (wr[:], "w_router")]
        ZB = dict(qk=0, v=1, og=2, lr=3, kT=4, qT=5, sc=6, o=7)
        bk = {n: psum[:, b, :] for n, b in ZB.items()}

        def rows(t, n):
            return t[bass.ds(n * P, P), :]

        block = ctx.enter_context(nc.Block())

        @block.sync
        def _(sp):
            def load_x(n, j):
                if late(n, 2):
                    sp.wait_ge(x_in[j], 8 * (n - j))
                sp.dma_start(xt[:, bass.ds(n, 1), :].rearrange("p a b -> p (a b)"), rows(a["x"], n)).then_inc(x_in[j], 16)

            load_x(0, 0)
            sp.dma_start(g1[:], a["g_mix"].to_broadcast([P, D])).then_inc(g1_in, 16)
            sp.dma_start(cst[:], a["consts"]).then_inc(g1_in, 16)
            load_x(1, 1)
            with sp.Fori(1, (NT - 1) // 2) as i:
                load_x(2 * i, 0)
                load_x(2 * i + 1, 1)
            load_x(NT - 1, 0)
            for c in range(CC):
                if c >= 2:
                    sp.wait_ge(cv_ps, 6 * (c - 1))
                sp.dma_start(wcv[c % 2], a["w_cv"][c]).then_inc(wcv_in[c % 2], 16)
                if c == 0:
                    for dst, name in SMALL:
                        sp.dma_start(dst, a[name]).then_inc(c_in, 16)
                    sp.dma_start(brb[:], a["b_router"].to_broadcast([P, G + NE])).then_inc(c_in, 16)
                    for cc in range(CC):
                        sp.dma_start(us[:, cc, :, 0:HIST], a["state_conv"][:, cc]).then_inc(hist_in, 16)
                if c == 1:
                    sp.wait_ge(xs_rdy, NT)
                    sp.dma_start(wtok, a["w_tok"]).then_inc(wtok_in, 16)
                    sp.wait_ge(zero, 1)
                    for half in range(2):
                        sp.dma_start(a["yrows"][NE * P:NTILE * P, half * 512:(half + 1) * 512].rearrange("(t p) w -> p t w", p=P),
                                     PT[:].rearrange("p a b -> p (a b)").unsqueeze(1).to_broadcast([P, EXTRA, 512])
                                     ).then_inc(y_zero, 16)
            sp.wait_ge(u_rdy, 2 * CC)
            sp.wait_ge(hist_in, 16 * CC)
            sp.dma_start(o["conv_prompt"], u[:, :, SEQ:SEQ + HIST]).then_inc(cst_out, 16)
            for c in range(CC):
                sp.dma_start(o["conv_sample"][:, c], us[:, c, :, TB:TB + HIST]).then_inc(cst_out, 16)
            sp.wait_ge(og_ps, NT)
            sp.dma_start(s0, a["state_gla"]).then_inc(s0_in, 16)
            sp.wait_ge(xTs_rdy, NT)
            sp.dma_start(wout, a["w_out"]).then_inc(wout_in, 16)
            sp.wait_ge(xs_rdy, NT)
            sp.dma_start(g1[:], a["g_ffn"].to_broadcast([P, D])).then_inc(g2_in, 16)
            sp.wait_ge(S_rdy, NT - 1)
            sp.dma_start(o["gla_prompt"], St[:]).then_inc(out_st, 16)
            sp.wait_ge(SU_out, NB)
            sp.dma_start(o["gla_sample"], s0).then_inc(out_st, 16)

            def mix_io(n, j):
                if not late(n, 1):
                    sp.wait_ge(og_ps, NT)
                if late(n, 2):
                    sp.wait_ge(h_rdy, n - 1)
                sp.dma_start(xTs[j][:].rearrange("p a b -> p (a b)"), rows(a["x"], n)).then_inc(x2_in[j], 16)

            def xn2_store(n, j):
                sp.wait_ge(xn2_rdy, n + 1)
                sp.dma_start(rows(a["xn2"], n), xn2[j]).then_inc(xn2_out[j], 16)

            mix_io(0, 0)
            mix_io(1, 1)
            with sp.Fori(1, (NT - 1) // 2) as i:
                for j in range(2):
                    xn2_store(2 * i + j - 2, j)
                    mix_io(2 * i + j, j)
            xn2_store(NT - 3, 0)
            mix_io(NT - 1, 0)
            xn2_store(NT - 2, 1)
            xn2_store(NT - 1, 0)
            sp.wait_ge(xn2_out[0], 16 * 5)
            sp.wait_ge(xn2_out[1], 16 * 4)

            def weights(t, sl):
                if late(t, 3):
                    sp.wait_ge(gu_ps, t - 2)
                elif t == 0:
                    sp.wait_ge(w_ps, 2 * NT)
                    sp.wait_ge(lg_ps, NT)
                sp.dma_start(wgu[sl], a["w_gu"][bass.ds(t, 1)].rearrange("a p k f -> (a p) k f")).then_inc(gu_in[sl], 16)
                if late(t, 3):
                    sp.wait_ge(y_ps, t - 2)
                sp.dma_start(wdn[sl], a["w_dn"][bass.ds(t, 1)].rearrange("a p k f -> (a p) k f")).then_inc(dn_in[sl], 16)

            def y_store(t, sl):
                sp.wait_ge(y_a, t + 1)
                sp.wait_ge(y_v, t + 1)
                sp.dma_start(rows(a["yrows"], t), yt[sl]).then_inc(y_out[sl], 16)

            weights(0, 0)
            weights(1, 1)
            weights(2, 2)

            def expert_io(t, sl):
                y_store(t, sl)
                weights(t + 3, sl)

            with sp.Fori(0, (NE - 5) // 3) as i:
                for sl in range(3):
                    expert_io(3 * i + sl, sl)
            expert_io(NE - 5, 0)
            expert_io(NE - 4, 1)
            y_store(NE - 3, 2)
            sp.wait_ge(pos_rdy, 1)
            count = sp.value_load(plan[0:1, EXTRA + 2:EXTRA + 3], min_val=0, max_val=EXTRA)

            def extra_weights(t, sl, done):
                e = sp.value_load(plan[0:1, bass.ds(t, 1)], min_val=0, max_val=NE - 1)
                sp.wait_ge(gu_ps, done)
                sp.dma_start(wgu[sl], a["w_gu"][bass.ds(e, 1)].rearrange("a p k f -> (a p) k f")).then_inc(gu_in[sl], 16)
                sp.wait_ge(y_ps, done)
                sp.dma_start(wdn[sl], a["w_dn"][bass.ds(e, 1)].rearrange("a p k f -> (a p) k f")).then_inc(dn_in[sl], 16)

            with sp.If(count > 0):
                extra_weights(0, 2, NE - 2)
            y_store(NE - 2, 0)
            with sp.If(count > 1):
                extra_weights(1, 1, NE)
            y_store(NE - 1, 1)
            sp.wait_ge(y_ps, NE)
            for k in range(6):
                sp.dma_start(wple[k], a["w_ple"][:, k]).then_inc(wple_in, 16)

            def extra_io(t, sl):
                with sp.If(count > t + 2):
                    extra_weights(t + 2, sl, t + NE + 1)
                y_store(t + NE, sl)
                sp.wait_ge(y_out[3 - sl], extra_turn(t - 1, 3 - sl))
                hold(sp, passed_sp)
                with sp.If(count == t + 1):
                    sp.wait_ge(y_out[sl], extra_turn(t, sl))
                    hold(sp, passed_sp)

            extra(sp, count, extra_io)
            for sl in range(3):
                sp.wait_ge(y_out[sl], 16 * ((NE + 2 - sl) // 3))
            sp.sem_inc(y_all, 1)

            sp.wait_ge(moe_done, 1)
            for k in range(6, KC):
                sp.dma_start(wple[k], a["w_ple"][:, k]).then_inc(wple_in, 16)
            sp.dma_start(wproj, a["w_proj"]).then_inc(pw_in, 16)
            sp.dma_start(gfin, a["g_final"].to_broadcast([P, D])).then_inc(pw_in, 16)
            sp.dma_start(g1[:], a["g_ple"].to_broadcast([P, D])).then_inc(pw_in, 16)

            def load_p(n, j):
                if late(n, 2):
                    sp.wait_ge(pr_ps, n - 1)
                sp.dma_start(pT[j], a["pT"][bass.ds(n, 1)].rearrange("a p k t -> (a p) k t")).then_inc(pT_in[j], 16)

            def y_final(n, j):
                sp.wait_ge(y_rdy, n + 1)
                sp.dma_start(rows(o["y"], n), yo[j]).then_inc(fin_out[j], 16)

            load_p(0, 0)
            load_p(1, 1)
            with sp.Fori(0, (NT - 3) // 2) as i:
                for j in range(2):
                    y_final(2 * i + j, j)
                    load_p(2 * i + j + 2, j)
            y_final(NT - 3, 0)
            load_p(NT - 1, 0)
            y_final(NT - 2, 1)
            y_final(NT - 1, 0)
            sp.wait_ge(fin_out[0], 16 * 5)
            sp.wait_ge(fin_out[1], 16 * 4)
            sp.wait_ge(out_st, 32)

        @block.gpsimd
        def _(pl):
            pl.memset(eps[:], EPS)
            pl.memset(PT[:], 0.0)
            pl.memset(u[:, :, 0:HIST], 0.0)
            pl.memset(lrT[:], 1.0)
            pl.memset(St[:], 0.0).then_inc(zero, 1)
            for c in range(CC):
                pl.wait_ge(cv_sb, 6 * (c + 1))
                pl.tensor_tensor(u[:, c, HIST:UW], a_sb[:, 0:SEQ], sg_sb[:, 0:SEQ], ALU.mult).then_inc(u_rdy, 1)
                pl.tensor_tensor(us[:, c, :, HIST:SW], a_sb[:, SEQ:SEQ + NS].rearrange("p (b t) -> p b t", t=TB),
                                 sg_sb[:, SEQ:SEQ + NS].rearrange("p (b t) -> p b t", t=TB), ALU.mult).then_inc(u_rdy, 1)
            pl.wait_ge(u_rdy, 2 * CC)
            pl.memset(oraw[NS:P, NT - 1, :], 0.0).then_inc(zero, 1)

            def copy_xT(n, j):
                if late(n, 2):
                    pl.wait_ge(og_ps, n - 1)
                pl.tensor_copy(xTs[j][:], xnT[:, :, bass.ds(n * P, P)]).then_inc(xTs_rdy, 1)

            def state_scaled(n, j):
                pl.wait_ge(E_rdy, n + 1)
                if late(n, 1):
                    pl.wait_ge(S_rdy, n)
                pl.wait_ge(xTs_rdy, min(n + 2, NT) if isinstance(n, int) else n + 2)
                pl.wait_ge(zero, 2)
                pl.tensor_tensor(Smid[:], St[:], EL[j][:, :, 0:1].to_broadcast([DK, H, DV]), ALU.mult).then_inc(Sm_rdy, 1)
                pl.wait_ge(Sm_rdy, 2 * n + 1)
                pl.tensor_tensor(Slast[:], Smid[:], EL[j][:, :, 1:2].to_broadcast([DK, H, DV]), ALU.mult).then_inc(Sm_rdy, 1)

            pl.wait_ge(xnT_a, NT)
            pl.wait_ge(xnT_v, NT)
            pl.wait_ge(zero, 2)
            copy_xT(0, 0)
            copy_xT(1, 1)
            def gla(n, j):
                state_scaled(n, j)
                pl.wait_ge(Sm_rdy, 2 * n + 2)
                copy_xT(n + 2, j)

            gla(0, 0)
            gla(1, 1)
            with pl.Fori(1, 3) as i:
                gla(2 * i, 0)
                gla(2 * i + 1, 1)
            gla(6, 0)
            state_scaled(7, 1)
            pl.wait_ge(og_ps, NT)
            pl.memset(qm, 0.0).then_inc(zero, 1)
            pl.wait_ge(zero, 3)
            pl.wait_ge(qT_rdy, NT)
            for hd in range(H):
                for b in range(NB):
                    pl.tensor_copy(qm[:, hd, b, b * TB:(b + 1) * TB], qkT[:, hd, b * TB:(b + 1) * TB])
            for b in range(NB):
                x = pl.tensor_scalar(km[:, b, :], qk[:, QW:2 * QW], C["seqone"][:, b:b + 1], None, ALU.mult)
            x.then_inc(smp, 1)

            def conv_tile(n, j):
                if late(n, 2):
                    pl.wait_ge(w_ps, 2 * n - 2)
                pl.tensor_copy(catT[j][:, CC:KC, :], cT[:, :, bass.ds(n * P, P)]).then_inc(catT_c, 1)

            pl.wait_ge(cT_rdy, CC)
            tiles(pl, conv_tile)

            pl.wait_ge(ids_rdy, 1)
            pl.wait_ge(xn2_out[0], 16 * 5)
            pl.wait_ge(xn2_out[1], 16 * 4)

            def gather(t, sl):
                if late(t, 3):
                    pl.wait_ge(xgT_ps, t - 2)
                pl.tensor_copy(idx[sl][:], ids[:, bass.ds(t, 1)]).then_inc(idx_rdy, 1)
                pl.wait_ge(idx_rdy, t + 1)
                hold(pl, passed)
                pl.indirect_dma_start(xg[sl], None, a["xn2"], bass.IndirectOffsetOnAxis(idx[sl][:], 0)).then_inc(xg_in[sl], 16)

            gather(0, 0)
            gather(1, 1)
            gather(2, 2)
            with pl.Fori(1, (NE - 2) // 3) as i:
                for sl in range(3):
                    gather(3 * i + sl, sl)
            gather(NE - 2, 0)
            gather(NE - 1, 1)
            count = pl.value_load(plan[0:1, EXTRA + 2:EXTRA + 3], min_val=0, max_val=EXTRA)

            def gather_extra(t, sl):
                pl.wait_ge(xgT_ps, t + NE - 1)
                pl.tensor_copy(idx[sl][:], ids[:, bass.ds(t + NE, 1)]).then_inc(idx_rdy, 1)
                pl.wait_ge(idx_rdy, t + NE + 1)
                hold(pl, passed)
                pl.indirect_dma_start(xg[sl], None, a["xn2"], bass.IndirectOffsetOnAxis(idx[sl][:], 0)).then_inc(xg_in[sl], 16)

            extra(pl, count, gather_extra)

            pl.wait_ge(y_all, 1)
            pl.wait_ge(moe_done, 1)

            def gather_y(n, j):
                if late(n, 2):
                    pl.wait_ge(add_rdy, 2 * n - 2)
                for m in range(2):
                    pl.tensor_copy(idy[j][m][:], posY[:, bass.ds(n + m * NT, 1)]).then_inc(idy_rdy, 1)
                    pl.wait_ge(idy_rdy, 2 * n + m + 1)
                    hold(pl, passed)
                    pl.indirect_dma_start(yg[j][m], None, a["yrows"],
                                          bass.IndirectOffsetOnAxis(idy[j][m][:], 0)).then_inc(yg_in[j][m], 16)

            tiles(pl, gather_y)

        @block.scalar
        def _(act):
            def norm_x(n, j):
                act.wait_ge(x_in[j], 8 * (n - j) + 16)
                act.activation(sqj[j], xt[:, bass.ds(n, 1), :].rearrange("p a b -> p (a b)"), ACT.Square, accum_out=ssq[:, j:j + 1]).then_inc(ssq_rdy, 1)
                act.wait_ge(ssq_rdy, n + 1)
                act.activation(std[:, j:j + 1], ssq[:, j:j + 1], ACT.Sqrt, scale=1.0 / D,
                               bias=eps[:, 0:1]).then_inc(std_rdy, 1)

            def evac_xT(n, j):
                act.wait_ge(xT_ps, n + 1)
                act.activation(xnT[:, 0:4, bass.ds(n * P, P)], psum[:, 4 + 2 * j, :].rearrange("p (a b) -> p a b", b=P),
                               ACT.Copy).then_inc(xnT_a, 1)

            act.wait_ge(zero, 1)
            norm_x(0, 0)
            norm_x(1, 1)
            with act.Fori(1, (NT - 1) // 2) as i:
                for j in range(2):
                    evac_xT(2 * i + j - 2, j)
                    norm_x(2 * i + j, j)
            evac_xT(NT - 3, 0)
            norm_x(NT - 1, 0)
            evac_xT(NT - 2, 1)
            evac_xT(NT - 1, 0)

            for c in range(CC):
                if c >= 1:
                    act.wait_ge(u_rdy, 2 * c)
                for part, (dst, fn) in enumerate([(sg_sb, ACT.Sigmoid), (a_sb, ACT.Copy)]):
                    for b in range(NBLK):
                        act.wait_ge(cv_ps, 6 * c + 3 * part + b + 1)
                        act.activation(dst[:, b * BLK:(b + 1) * BLK], psum[:, 3 * part + b, 0:BLK], fn).then_inc(cv_sb, 1)

            def lr_out(n):
                act.wait_ge(lr_ps, n + 1)
                act.activation(lr_sb[:], bk["lr"][:, 0:LR], ACT.Copy).then_inc(lr_rdy, 1)

            def lrT_out(n):
                act.wait_ge(lrT_ps, n + 1)
                act.activation(lrT[0:LR, :], bk["lr"][0:LR, LR:LR + P], ACT.Copy).then_inc(lrT_rdy, 1)

            def log_gate(n):
                act.wait_ge(lap_ps, n + 1)
                act.activation(absx[:], bk["lr"][:, 144:400], ACT.Abs).then_inc(absx_rdy, 1)
                act.wait_ge(absx_rdy, 3 * n + 1)
                act.activation(absx[:], absx[:], ACT.Exp, scale=-1.0).then_inc(absx_rdy, 1)
                act.wait_ge(absx_rdy, 3 * n + 2)
                act.activation(absx[:], absx[:], ACT.Ln, bias=1.0).then_inc(absx_rdy, 1)

            def v_out(n, j):
                act.wait_ge(v_ps, n + 1)
                if late(n, 2):
                    act.wait_ge(U_ps, n - 1)
                act.activation(v_sb[j][:], bk["v"], ACT.Copy).then_inc(v_rdy, 1)

            def decays(n, j):
                act.wait_ge(b_ps, n + 1)
                act.activation(E1[:], bk["lr"][:, 144:400], ACT.Exp)
                act.activation(E2[:], bk["lr"][:, 144:400], ACT.Exp, scale=-1.0)
                if isinstance(n, int) and n == NT - 1:
                    x = act.activation(ELs[:].rearrange("p h b -> p (h b)"), bk["lr"][0:DK, 400:400 + H * NB], ACT.Exp)
                else:
                    if late(n, 2):
                        act.wait_ge(S_rdy, n - 1)
                    x = act.activation(EL[j][:].rearrange("p h b -> p (h b)"), bk["lr"][0:DK, 400:400 + 2 * H], ACT.Exp)
                x.then_inc(E_rdy, 1)

            def gate_tanh(n):
                act.wait_ge(og_ps, n + 1)
                if late(n, 1):
                    act.wait_ge(gog_rdy, n)
                act.activation(th[:], bk["og"], ACT.Tanh, scale=0.5).then_inc(th_rdy, 1)

            def kT_out(n):
                act.wait_ge(qkT_ps, n + 1)
                act.activation(qkT[:, H:2 * H, :], bk["kT"][0:DK, :].rearrange("p (a b) -> p a b", b=P),
                               ACT.Copy).then_inc(kT_rdy, 1)

            def o_out(n, m=P):
                act.wait_ge(o_ps, n + 1)
                act.activation(oraw[0:m, bass.ds(n, 1), :], bk["o"][0:m, :].rearrange("p (a b) -> p a b", a=1),
                               ACT.Copy).then_inc(o_rdy, 1)

            def gla(n, j):
                lr_out(n + 1)
                kT_out(n)
                lrT_out(n + 1)
                log_gate(n + 1)
                v_out(n + 1, 1 - j)
                decays(n + 1, 1 - j)
                o_out(n)
                gate_tanh(n + 1)

            lr_out(0)
            lrT_out(0)
            log_gate(0)
            v_out(0, 0)
            decays(0, 0)
            gate_tanh(0)
            gla(0, 0)
            with act.Fori(0, 3) as i:
                gla(2 * i + 1, 1)
                gla(2 * i + 2, 0)
            gla(NT - 2, 1)
            kT_out(NT - 1)

            def o_square(n, j):
                for hd in range(H):
                    x = act.activation(th[:, hd * DV:(hd + 1) * DV], oraw[:, bass.ds(n, 1), hd * DV:(hd + 1) * DV]
                                       .rearrange("p a b -> p (a b)"), ACT.Square,
                                       accum_out=osq[:, j, hd:hd + 1])
                x.then_inc(osq_rdy, 1)
                act.wait_ge(osq_rdy, n + 1)
                act.activation(ostd[:, j, :], osq[:, j, :], ACT.Sqrt, scale=1.0 / DV,
                               bias=eps[:, 0:1]).then_inc(ostd_rdy, 1)

            for c in range(CC):
                if c == 0:
                    act.wait_ge(conv, 2 * K * CC)
                    act.wait_ge(cst_out, 16 * (CC + 1))
                act.activation(csq[:, c, :], cT[:, c, :], ACT.Square).then_inc(csq_rdy, 1)
            act.wait_ge(ln_v, 3)
            act.activation(rstdb, rstdb, ACT.Sqrt, bias=eps[:, 0:1]).then_inc(ln_std, 1)
            act.wait_ge(gog_rdy, NT)
            o_square(0, 0)
            for c in range(CC):
                act.wait_ge(ln_x, 2 * (c + 1))
                act.activation(cT[:, c, :], cT[:, c, :], ACT.Silu, scale=cvec[:, 1, c:c + 1],
                               bias=cvec[:, 2, c:c + 1]).then_inc(cT_rdy, 1)

            def oT_out(n, j):
                act.wait_ge(oT_ps, n + 1)
                act.activation(catT[j][:, 0:H, :], psum[:, 4, :].rearrange("p (a b) -> p a b", b=P), ACT.Copy,
                               scale=gghalf[:, 0:1]).then_inc(catT_o, 1)

            def xn2T_out(n, j):
                act.wait_ge(xn2T_ps, n + 1)
                act.activation(xn2T[j][:, 0:4, :], psum[:, 5, :].rearrange("p (a b) -> p a b", b=P),
                               ACT.Copy).then_inc(xn2T_a, 1)

            def h_square(n, j):
                act.wait_ge(h_rdy, n + 1)
                if late(n, 2):
                    act.wait_ge(xn2_out[j], 8 * (n - j))
                act.activation(xn2[j], h[:, bass.ds(n, 1), :].rearrange("p a b -> p (a b)"), ACT.Square,
                               accum_out=ssq[:, j:j + 1]).then_inc(ssq2_rdy, 1)
                act.wait_ge(ssq2_rdy, n + 1)
                act.activation(std[:, j:j + 1], ssq[:, j:j + 1], ACT.Sqrt, scale=1.0 / D,
                               bias=eps[:, 0:1]).then_inc(std2_rdy, 1)

            def mix(n, j):
                last = isinstance(n, int) and n == NT - 1
                if not last:
                    o_square(n + 1, 1 - j)
                if late(n, 1):
                    xn2T_out(n - 1, 1 - j)
                if not last:
                    oT_out(n + 1, 1 - j)
                h_square(n, j)

            o_out(NT - 1, NS)
            oT_out(0, 0)
            tiles(act, mix)
            xn2T_out(NT - 1, 0)

            act.wait_ge(gd_rdy, 1)
            act.activation(gsc, gd, ACT.Exp).then_inc(ge_rdy, 1)
            act.wait_ge(dv_rdy, 1)
            act.activation(one["ev"], one["dv"], ACT.Exp).then_inc(ev_rdy, 1)

            def halfT(dst, bank, sem_):
                act.activation(dst[:, 0:4, :], psum[:, bank, :].rearrange("p (a b) -> p a b", b=P), ACT.Copy).then_inc(sem_, 1)

            def xgT_out(t, sl):
                act.wait_ge(xgT_ps, t + 1)
                halfT(xgT[sl], 0, xgT_a)

            def silu(t, sl):
                act.wait_ge(gu_ps, t + 1)
                if late(t, 3):
                    act.wait_ge(hg_rdy, t - 2)
                act.activation(sil[sl], psum[:, 2 + sl, 0:FF], ACT.Silu).then_inc(sil_rdy, 1)

            def y_half(t, sl, stored=None):
                act.wait_ge(y_ps, t + 1)
                if stored is not None or late(t, 3):
                    act.wait_ge(y_out[sl], turn_of(t, sl) * 16 if stored is None else stored)
                act.activation(yt[sl][:, 0:512], psum[:, 6, :], ACT.Copy).then_inc(y_a, 1)

            def expert(t, sl):
                silu(t, sl)
                if isinstance(t, int) and t == NE - 1:
                    with act.If(count > 0):
                        xgT_out(NE, 2)
                else:
                    xgT_out(t + 1, (sl + 1) % 3)
                if late(t, 1):
                    y_half(t - 1, (sl - 1) % 3)

            act.wait_ge(pos_rdy, 1)
            count = act.value_load(plan[0:1, EXTRA + 2:EXTRA + 3], min_val=0, max_val=EXTRA)
            xgT_out(0, 0)
            experts(act, expert)
            with act.If(count == 0):
                y_half(NE - 1, (NE - 1) % 3)

            def expert_extra(t, sl):
                act.wait_ge(gu_ps, t + NE + 1)
                act.wait_ge(hg_rdy, t + NE - 1)
                act.activation(sil[sl], psum[:, 2 + sl, 0:FF], ACT.Silu).then_inc(sil_rdy, 1)
                with act.If(count > t + 1):
                    xgT_out(t + NE + 1, 3 - sl)
                y_half(t + NE - 1, 3 - sl, extra_turn(t - 1, 3 - sl) - 16)
                with act.If(count == t + 1):
                    y_half(t + NE, sl, extra_turn(t, sl) - 16)

            extra(act, count, expert_extra)

            def h_square3(n, j):
                act.wait_ge(add_rdy, 2 * n + 2)
                act.activation(xn3[j], h[:, bass.ds(n, 1), :].rearrange("p a b -> p (a b)"), ACT.Square,
                               accum_out=ssq[:, j:j + 1]).then_inc(ssq3_rdy, 1)
                act.wait_ge(ssq3_rdy, n + 1)
                act.activation(std[:, j:j + 1], ssq[:, j:j + 1], ACT.Sqrt, scale=1.0 / D,
                               bias=eps[:, 0:1]).then_inc(std3_rdy, 1)

            def x3T_out(n, j):
                act.wait_ge(x3T_ps, n + 1)
                halfT(x3T[j], 0, x3T_a)

            def gate_sig(n, j):
                act.wait_ge(gt_ps, 2 * n + 2)
                if late(n, 2):
                    act.wait_ge(y_rdy, n - 1)
                act.activation(mixd[j].rearrange("p (a b) -> p a b", b=512), psum[:, 2 + 4 * j:4 + 4 * j, :],
                               ACT.Sigmoid).then_inc(sg_rdy, 1)

            def out_square(n, j):
                act.wait_ge(mix_rdy, 2 * n + 2)
                if late(n, 2):
                    act.wait_ge(fin_out[j], 8 * (n - j))
                act.activation(yo[j], mixd[j], ACT.Square, accum_out=ssq[:, j:j + 1]).then_inc(ssq4_rdy, 1)
                act.wait_ge(ssq4_rdy, n + 1)
                act.activation(std[:, j:j + 1], ssq[:, j:j + 1], ACT.Sqrt, scale=1.0 / D,
                               bias=eps[:, 0:1]).then_inc(std4_rdy, 1)

            def embed(n, j):
                if not (isinstance(n, int) and n == NT - 1):
                    x3T_out(n + 1, 1 - j)
                if not (isinstance(n, int) and n >= NT - 2):
                    h_square3(n + 2, j)
                gate_sig(n, j)
                out_square(n, j)

            act.wait_ge(moe_done, 1)
            h_square3(0, 0)
            h_square3(1, 1)
            x3T_out(0, 0)
            embeds(act, embed)

        @block.vector
        def _(dve):
            dve.wait_ge(g1_in, 32)

            def norm_x(n, j):
                dve.wait_ge(std_rdy, n + 1)
                dve.reciprocal(rst[:, j:j + 1], std[:, j:j + 1]).then_inc(rst_rdy, 1)
                dve.wait_ge(rst_rdy, n + 1)
                if late(n, 2):
                    dve.wait_ge(xT_ps, n - 1)
                dve.scalar_tensor_tensor(xs[j], xt[:, bass.ds(n, 1), :].rearrange("p a b -> p (a b)"), rst[:, j:j + 1], g1[:], ALU.mult, ALU.mult).then_inc(xs_rdy, 1)

            def evac_xT(n, j):
                dve.wait_ge(xT_ps, n + 1)
                dve.tensor_copy(xnT[:, 4:8, bass.ds(n * P, P)],
                                psum[:, 5 + 2 * j, :].rearrange("p (a b) -> p a b", b=P)).then_inc(xnT_v, 1)

            norm_x(0, 0)
            norm_x(1, 1)
            with dve.Fori(1, (NT - 1) // 2) as i:
                for j in range(2):
                    evac_xT(2 * i + j - 2, j)
                    norm_x(2 * i + j, j)
            evac_xT(NT - 3, 0)
            norm_x(NT - 1, 0)
            evac_xT(NT - 2, 1)
            evac_xT(NT - 1, 0)
            dve.wait_ge(c_in, 16 * (len(SMALL) + 1))
            dve.tensor_scalar(gghalf[:], ggo[:], 0.5, None, ALU.mult)

            dve.wait_ge(zero, 1)
            dve.wait_ge(hist_in, 16 * CC)
            def taps(c, first, count):
                w = wc[:, bass.ds(c, 1), :].rearrange("p a k -> p (a k)")
                acc = cT[:, bass.ds(c, 1), 0:SEQ].rearrange("p a t -> p (a t)")
                accs = cT[:, bass.ds(c, 1), SEQ:SEQ + NS].rearrange("p a (b t) -> p (a b) t", t=TB)
                for k in range(first, min(first + count, K)):
                    src = u[:, bass.ds(c, 1), k:k + SEQ].rearrange("p a t -> p (a t)")
                    srcs = us[:, bass.ds(c, 1), :, k:k + TB].rearrange("p a b t -> p (a b) t")
                    if k == 0:
                        dve.wait_ge(u_rdy, 2 * (c + 1))
                        b = cvec[:, 0, bass.ds(c, 1)]
                        dve.tensor_scalar(acc, src, w[:, 0:1], b, ALU.mult, ALU.add).then_inc(conv, 1)
                        dve.tensor_scalar(accs, srcs, w[:, 0:1], b, ALU.mult, ALU.add).then_inc(conv, 1)
                    else:
                        dve.wait_ge(conv, 2 * K * c + 2 * k - 1)
                        dve.scalar_tensor_tensor(acc, src, w[:, k:k + 1], acc, ALU.mult, ALU.add).then_inc(conv, 1)
                        dve.wait_ge(conv, 2 * K * c + 2 * k)
                        dve.scalar_tensor_tensor(accs, srcs, w[:, k:k + 1], accs, ALU.mult, ALU.add).then_inc(conv, 1)

            dve.memset(cT[:, :, SEQ + NS:TOK], 0.0)
            with dve.Fori(0, CC // 2) as c:
                taps(c, 0, K)

            def log_gate(n):
                dve.wait_ge(absx_rdy, 3 * n + 3)
                dve.scalar_tensor_tensor(la[:], bk["lr"][:, 144:400], 0.0, absx[:], ALU.min, ALU.subtract).then_inc(la_rdy, 1)

            def decay_qk(n):
                dve.wait_ge(E_rdy, n + 1)
                dve.wait_ge(qk_ps, n + 1)
                dve.scalar_tensor_tensor(qk[:, 0:QW], bk["qk"][:, 0:QW], DK ** -0.5, E1[:], ALU.mult, ALU.mult)
                dve.tensor_tensor(qk[:, QW:2 * QW], bk["qk"][:, QW:2 * QW], E2[:], ALU.mult).then_inc(qk_rdy, 1)

            def gate(n):
                dve.wait_ge(th_rdy, n + 1)
                dve.scalar_tensor_tensor(gog[:, bass.ds(n, 1), :].rearrange("p a b -> p (a b)"), th[:], 1.0, bk["og"],
                                         ALU.add, ALU.mult).then_inc(gog_rdy, 1)

            def qT_out(n):
                dve.wait_ge(qkT_ps, n + 1)
                dve.tensor_copy(qkT[:, 0:H, :], bk["qT"][0:DK, :].rearrange("p (a b) -> p a b", b=P)).then_inc(qT_rdy, 1)

            def mask_scores(n, m):
                dve.wait_ge(sc_ps, n + 1)
                dve.tensor_tensor(PT[:], bk["sc"].rearrange("p (a b) -> p a b", b=P),
                                  m.unsqueeze(1).to_broadcast([P, H, P]), ALU.mult).then_inc(PT_rdy, 1)

            def state(n, j):
                dve.wait_ge(U_ps, n + 1)
                dve.wait_ge(Sm_rdy, 2 * n + 2)
                for hd in range(H):
                    x = dve.scalar_tensor_tensor(St[:, hd, :], bk["qT"][0:DK, hd * DV:(hd + 1) * DV], EL[j][:, hd, 1:2],
                                                 Slast[:, hd, :], ALU.mult, ALU.add)
                x.then_inc(S_rdy, 1)

            dve.wait_ge(y_zero, 32)

            def gla(n, j, c, first):
                qT_out(n)
                taps(c, first, 3)
                mask_scores(n, C["cmask"])
                log_gate(n + 1)
                taps(c, first + 3, 2)
                state(n, j)
                decay_qk(n + 1)
                taps(c, first + 5, 3)
                gate(n + 1)

            log_gate(0)
            decay_qk(0)
            gate(0)
            with dve.Fori(0, 2) as i:
                for r in range(4):
                    gla(4 * i + r, r % 2, i + CC // 2, 8 * r)
            qT_out(NT - 1)
            mask_scores(NT - 1, C["cmasks"])
            dve.wait_ge(st_ps, 1)
            dve.tensor_scalar(mean.rearrange("p (a b) -> p a b", b=BLK), psum[:, 0:3, 0:BLK], 1.0 / CW, None,
                              ALU.mult).then_inc(ln_v, 1)
            dve.wait_ge(ln_v, 1)
            dve.tensor_tensor(csq[:, 0, :], mean, mean, ALU.mult).then_inc(ln_v, 1)
            dve.wait_ge(ln_v, 2)
            dve.scalar_tensor_tensor(rstdb.rearrange("p (a b) -> p a b", b=BLK), psum[:, 3:6, 0:BLK], 1.0 / CW,
                                     csq[:, 0, :].rearrange("p (a b) -> p a b", b=BLK), ALU.mult, ALU.subtract).then_inc(ln_v, 1)
            dve.tensor_tensor(cT[:, 0, :], cT[:, 0, :], mean, ALU.subtract).then_inc(ln_x, 1)
            dve.wait_ge(ln_std, 1)
            dve.reciprocal(rstdb, rstdb).then_inc(ln_v, 1)
            dve.wait_ge(ln_v, 4)
            for c in range(CC):
                dve.wait_ge(ln_x, 2 * c + 1)
                dve.tensor_tensor(cT[:, c, :], cT[:, c, :], rstdb, ALU.mult).then_inc(ln_x, 1)
                if c + 1 < CC:
                    dve.tensor_tensor(cT[:, c + 1, :], cT[:, c + 1, :], mean, ALU.subtract).then_inc(ln_x, 1)

            dve.wait_ge(s0_in, 16)
            for b in range(NB):
                dve.wait_ge(SU_ps, b + 1)
                dve.tensor_tensor(s0[:, b], psum[0:DK, b % 6, :].rearrange("p (h d) -> p h d", d=DV), s0[:, b],
                                  ALU.add).then_inc(SU_add, 1)
            for b in range(NB):
                dve.wait_ge(SU_add, b + 1)
                dve.tensor_tensor(s0[:, b], s0[:, b], ELs[:, :, b:b + 1].to_broadcast([DK, H, DV]), ALU.mult).then_inc(SU_out, 1)

            def o_norm(n, j):
                dve.wait_ge(ostd_rdy, n + 1)
                dve.reciprocal(orst[:, j, :], ostd[:, j, :]).then_inc(orst_rdy, 1)
                dve.wait_ge(orst_rdy, n + 1)
                if late(n, 2):
                    dve.wait_ge(oT_ps, n - 1)
                for hd in range(H):
                    cols = slice(hd * DV, (hd + 1) * DV)
                    x = dve.scalar_tensor_tensor(og[j][:, cols], oraw[:, bass.ds(n, 1), cols].rearrange("p a b -> p (a b)"),
                                                 orst[:, j, hd:hd + 1],
                                                 gog[:, bass.ds(n, 1), cols].rearrange("p a b -> p (a b)"), ALU.mult, ALU.mult)
                x.then_inc(og_rdy, 1)

            def norm_h(n, j):
                dve.wait_ge(std2_rdy, n + 1)
                dve.reciprocal(rst[:, j:j + 1], std[:, j:j + 1]).then_inc(rst2_rdy, 1)
                dve.wait_ge(rst2_rdy, n + 1)
                dve.scalar_tensor_tensor(xn2[j], h[:, bass.ds(n, 1), :].rearrange("p a b -> p (a b)"), rst[:, j:j + 1],
                                         g1[:], ALU.mult, ALU.mult).then_inc(xn2_rdy, 1)

            def xn2T_out(n, j):
                dve.wait_ge(xn2T_ps, n + 1)
                dve.tensor_copy(xn2T[j][:, 4:8, :], psum[:, 6, :].rearrange("p (a b) -> p a b", b=P)).then_inc(xn2T_v, 1)

            def residual(n, j):
                dve.wait_ge(x2_in[j], 8 * (n - j) + 16)
                dve.wait_ge(w_ps, 2 * n + 2)
                dve.tensor_tensor(h[:, bass.ds(n, 1), :].rearrange("p a b -> p (a b)"),
                                  psum[:, 2 * j:2 * j + 2, :].rearrange("p a b -> p (a b)"),
                                  xTs[j][:].rearrange("p a b -> p (a b)"), ALU.add).then_inc(h_rdy, 1)

            def logit(n):
                dve.wait_ge(lg_ps, n + 1)
                dve.tensor_tensor(logits[:, bass.ds(n, 1), :].rearrange("p a b -> p (a b)"), psum[:, 7, 0:G + NE], brb[:],
                                  ALU.add).then_inc(lg_rdy, 1)

            dve.wait_ge(g2_in, 16)
            dve.wait_ge(out_st, 32)

            def mix(n, j):
                if late(n, 1):
                    norm_h(n - 1, 1 - j)
                if not (isinstance(n, int) and n == NT - 1):
                    o_norm(n + 1, 1 - j)
                if late(n, 1):
                    xn2T_out(n - 1, 1 - j)
                residual(n, j)
                if late(n, 1):
                    logit(n - 1)

            o_norm(0, 0)
            tiles(dve, mix)
            norm_h(NT - 1, 0)
            xn2T_out(NT - 1, 0)
            logit(NT - 1)

            steps = [0]

            def step(x):
                steps[0] += 1
                x.then_inc(rt, 1)
                dve.wait_ge(rt, steps[0])

            def over(v, n):
                return v.unsqueeze(len(v.shape)).to_broadcast([*v.shape, n])

            def first_max(src, m, ranks, sc, pick, w):
                step(dve.tensor_reduce(m, src, AX, ALU.max))
                step(dve.tensor_tensor(sc, src, over(m, w), ALU.is_equal))
                step(dve.tensor_tensor(sc, sc, C[ranks].unsqueeze(1).to_broadcast([P, NT, w]), ALU.mult))
                step(dve.tensor_reduce(pick, sc, AX, ALU.max))

            gl, el = logits[:, :, 0:G], logits[:, :, G:G + NE].rearrange("p n (g e) -> p n g e", e=E)
            dve.wait_ge(lg_rdy, NT)
            dve.wait_ge(xn2_out[0], 16 * 5)
            dve.wait_ge(xn2_out[1], 16 * 4)
            dve.wait_ge(lg_ps, NT)
            first_max(gl, one["gmax"], "desc4", gsc, one["gm"], G)
            step(dve.tensor_tensor(ohg, gsc, over(one["gm"], G), ALU.is_equal))
            dve.tensor_tensor(gd, gl, over(one["gmax"], G), ALU.subtract).then_inc(gd_rdy, 1)
            gsel = prod[:, 0:NT, :].rearrange("p n (g e) -> p n g e", e=E)
            step(dve.tensor_tensor(gsel, el, over(ohg, E), ALU.mult))
            step(dve.tensor_reduce(sel, gsel.rearrange("p n g e -> p n e g"), AX, ALU.add))
            first_max(sel, one["v1"], "desc8", esc, one["m1"], E)
            step(dve.tensor_tensor(oh[0], esc, over(one["m1"], E), ALU.is_equal))
            step(dve.scalar_tensor_tensor(sel, oh[0], -BIG, sel, ALU.mult, ALU.add))
            first_max(sel, one["v2"], "desc8", esc, one["m2"], E)
            step(dve.tensor_tensor(oh[1], esc, over(one["m2"], E), ALU.is_equal))
            dve.tensor_tensor(one["dv"], one["v2"], one["v1"], ALU.subtract).then_inc(dv_rdy, 1)
            for m in range(2):
                for g in range(G):
                    x = dve.tensor_tensor(M12[:, m, :, g * E:(g + 1) * E], oh[m], ohg[:, :, g:g + 1].to_broadcast([P, NT, E]),
                                          ALU.mult)
            step(x)
            step(dve.memset(M12[NS:P, :, NT - 1, :], 0.0))
            dve.tensor_tensor(Msum, M12[:, 0], M12[:, 1], ALU.add).then_inc(M_rdy, 1)
            dve.wait_ge(ge_rdy, 1)
            step(dve.tensor_reduce(one["gsum"], gsc, AX, ALU.add))
            step(dve.reciprocal(one["gw"], one["gsum"]))
            dve.wait_ge(ev_rdy, 1)
            step(dve.tensor_scalar(one["gm"], one["ev"], 1.0, None, ALU.add))
            step(dve.reciprocal(one["gm"], one["gm"]))
            step(dve.tensor_tensor(w12[:, 0, :], one["gm"], one["gw"], ALU.mult))
            step(dve.tensor_tensor(w12[:, 1, :], w12[:, 0, :], one["ev"], ALU.mult))
            step(dve.memset(before[:, 0, :], 0.0))
            dve.wait_ge(rk_ps, 1)
            for n in range(NT):
                step(dve.tensor_tensor(before[:, n + 1, :], before[:, n, :], psum[:, 1, n * NE:(n + 1) * NE], ALU.add))
            step(dve.tensor_tensor(rank, psum[:, 0, 0:NT * NE].rearrange("p (a b) -> p a b", b=NE), before[:, 0:NT, :], ALU.add))
            step(dve.tensor_tensor(cmpe, over(before[:, NT, :], E), C["steps"].unsqueeze(1).to_broadcast([P, NE, E]), ALU.is_gt))
            step(dve.tensor_reduce(nx, cmpe, AX, ALU.add))
            step(dve.memset(ovb, 0.0))
            step(dve.tensor_tensor_scan(inc, nx, ovb, 0.0, ALU.add, ALU.add))
            step(dve.tensor_tensor(ovb, inc, nx, ALU.subtract))
            step(dve.tensor_tensor(cmpt, inc.unsqueeze(1).to_broadcast([P, EXTRA, NE]), over(C["tidx"], NE), ALU.is_le))
            step(dve.tensor_reduce(et, cmpt, AX, ALU.add))
            step(dve.tensor_scalar(plan[:, 0:EXTRA], et, float(NE - 1), None, ALU.min))
            step(dve.tensor_copy(plan[:, EXTRA + 2:EXTRA + 3], inc[:, NE - 1:NE]))
            for name, v in [("rank", rank), ("exp", C["eidx"].unsqueeze(1).to_broadcast([P, NT, NE])),
                            ("ovb", ovb.unsqueeze(1).to_broadcast([P, NT, NE]))]:
                for m in range(2):
                    step(dve.tensor_tensor(prod[:, m * NT:(m + 1) * NT, :], M12[:, m], v, ALU.mult))
                step(dve.tensor_reduce(two[name], prod, AX, ALU.add))
            step(dve.tensor_tensor(cmpr, over(two["rank"], E), C["steps"].unsqueeze(1).to_broadcast([P, 2 * NT, E]), ALU.is_ge))
            step(dve.tensor_reduce(two["q"], cmpr, AX, ALU.add))
            step(dve.tensor_scalar(two["isq"], two["q"], 1.0, None, ALU.is_ge))
            step(dve.tensor_tensor(two["t"], two["ovb"], two["q"], ALU.add))
            step(dve.scalar_tensor_tensor(two["t"], two["t"], float(NE - 1), two["exp"], ALU.add, ALU.subtract))
            step(dve.tensor_tensor(two["t"], two["t"], two["isq"], ALU.mult))
            step(dve.tensor_tensor(two["t"], two["t"], two["exp"], ALU.add))
            step(dve.scalar_tensor_tensor(two["r"], two["q"], -float(P), two["rank"], ALU.mult, ALU.add))
            step(dve.scalar_tensor_tensor(two["fy"], two["t"], float(P), two["r"], ALU.mult, ALU.add))
            step(dve.tensor_tensor(oht, over(two["t"], NTILE), C["count"][:, 0:NTILE].unsqueeze(1)
                                   .to_broadcast([P, 2 * NT, NTILE]), ALU.is_equal))
            for m in range(2):
                t = slice(m * NT, (m + 1) * NT)
                dve.tensor_tensor(oht[:, t], oht[:, t], over(C["token"], NTILE), ALU.mult)
                dve.tensor_tensor(ohr[:, t], over(two["r"][:, t], P), C["count"].unsqueeze(1).to_broadcast([P, NT, P]),
                                  ALU.is_equal).then_inc(oh_rdy, 1)
            dve.tensor_copy(posY[:], two["fy"]).then_inc(pos_rdy, 1)
            dve.wait_ge(ids_ps, 1)
            dve.tensor_copy(ids[:], psum[:, 2, 0:NTILE]).then_inc(ids_rdy, 1)

            def halfT(dst, bank, sem_):
                dve.tensor_copy(dst[:, 4:8, :], psum[:, bank, :].rearrange("p (a b) -> p a b", b=P)).then_inc(sem_, 1)

            def xgT_out(t, sl):
                dve.wait_ge(xgT_ps, t + 1)
                halfT(xgT[sl], 1, xgT_v)

            def glu(t, sl):
                dve.wait_ge(sil_rdy, t + 1)
                dve.tensor_tensor(hg, sil[sl], psum[:, 2 + sl, FF:2 * FF], ALU.mult).then_inc(hg_rdy, 1)

            def hT_out(t):
                dve.wait_ge(hT_ps, t + 1)
                dve.tensor_copy(hT, psum[:, 5, 0:FF].rearrange("p (a b) -> p a b", b=P)).then_inc(hT_rdy, 1)

            def y_half(t, sl, stored=None):
                dve.wait_ge(y_ps, t + 1)
                if stored is not None or late(t, 3):
                    dve.wait_ge(y_out[sl], turn_of(t, sl) * 16 if stored is None else stored)
                dve.tensor_copy(yt[sl][:, 512:D], psum[:, 7, :]).then_inc(y_v, 1)

            def expert(t, sl):
                glu(t, sl)
                if isinstance(t, int) and t == NE - 1:
                    with dve.If(count > 0):
                        xgT_out(NE, 2)
                else:
                    xgT_out(t + 1, (sl + 1) % 3)
                if late(t, 1):
                    y_half(t - 1, (sl - 1) % 3)
                hT_out(t)

            count = dve.value_load(plan[0:1, EXTRA + 2:EXTRA + 3], min_val=0, max_val=EXTRA)
            xgT_out(0, 0)
            experts(dve, expert)
            with dve.If(count == 0):
                y_half(NE - 1, (NE - 1) % 3)

            def expert_extra(t, sl):
                glu(t + NE, sl)
                with dve.If(count > t + 1):
                    xgT_out(t + NE + 1, 3 - sl)
                y_half(t + NE - 1, 3 - sl, extra_turn(t - 1, 3 - sl) - 16)
                hT_out(t + NE)
                with dve.If(count == t + 1):
                    y_half(t + NE, sl, extra_turn(t, sl) - 16)

            extra(dve, count, expert_extra)

            def flat(n):
                return h[:, bass.ds(n, 1), :].rearrange("p a b -> p (a b)")

            def combine(n, j):
                for m in range(2):
                    dve.wait_ge(yg_in[j][m], 8 * (n - j) + 16)
                    if m:
                        dve.wait_ge(add_rdy, 2 * n + 1)
                    dve.scalar_tensor_tensor(flat(n), yg[j][m], w12[:, m, bass.ds(n, 1)], flat(n), ALU.mult,
                                             ALU.add).then_inc(add_rdy, 1)
                dve.wait_ge(std3_rdy, n + 1)
                dve.reciprocal(rst[:, j:j + 1], std[:, j:j + 1]).then_inc(rst3_rdy, 1)
                dve.wait_ge(rst3_rdy, n + 1)
                dve.scalar_tensor_tensor(xn3[j], flat(n), rst[:, j:j + 1], g1[:], ALU.mult, ALU.mult).then_inc(xn3_rdy, 1)

            def x3T_out(n, j):
                dve.wait_ge(x3T_ps, n + 1)
                halfT(x3T[j], 1, x3T_v)

            def finish(n, j):
                dve.wait_ge(sg_rdy, n + 1)
                dve.wait_ge(pr_ps, n + 1)
                dve.tensor_tensor(mixd[j], mixd[j], psum[:, 4:6, :].rearrange("p a b -> p (a b)"), ALU.mult).then_inc(mix_rdy, 1)
                dve.wait_ge(mix_rdy, 2 * n + 1)
                dve.tensor_tensor(mixd[j], mixd[j], flat(n), ALU.add).then_inc(mix_rdy, 1)
                dve.wait_ge(std4_rdy, n + 1)
                dve.reciprocal(rst[:, j:j + 1], std[:, j:j + 1]).then_inc(rst4_rdy, 1)
                dve.wait_ge(rst4_rdy, n + 1)
                dve.scalar_tensor_tensor(yo[j], mixd[j], rst[:, j:j + 1], gfin, ALU.mult, ALU.mult).then_inc(y_rdy, 1)

            def embed(n, j):
                if not (isinstance(n, int) and n == NT - 1):
                    x3T_out(n + 1, 1 - j)
                if not (isinstance(n, int) and n >= NT - 2):
                    combine(n + 2, j)
                finish(n, j)

            dve.wait_ge(pw_in, 48)
            combine(0, 0)
            combine(1, 1)
            x3T_out(0, 0)
            embeds(dve, embed)

        @block.tensor
        def _(pe):
            ident = C["ident"]
            pe.wait_ge(g1_in, 32)

            def transpose_x(n, j):
                pe.wait_ge(xs_rdy, n + 1)
                if late(n, 2):
                    pe.wait_ge(xnT_a, n - 1)
                    pe.wait_ge(xnT_v, n - 1)
                for k in range(KC):
                    x = pe.transpose(psum[:, 4 + 2 * j + k // 4, (k % 4) * P:(k % 4 + 1) * P], xs[j][:, k * P:(k + 1) * P], ident)
                x.then_inc(xT_ps, 1)

            tiles(pe, transpose_x)
            pe.wait_ge(xnT_a, NT)
            pe.wait_ge(xnT_v, NT)

            for c in range(CC):
                pe.wait_ge(wcv_in[c % 2], 16 * (c // 2 + 1))
                for part, col in enumerate([P, 0]):
                    for b in range(NBLK):
                        if c >= 1:
                            pe.wait_ge(cv_sb, 6 * (c - 1) + 3 * part + b + 1)
                        for k in range(KC):
                            x = pe.matmul(psum[:, 3 * part + b, 0:BLK], wcv[c % 2][:, k, col:col + P],
                                          xnT[:, k, b * BLK:(b + 1) * BLK], start=k == 0, stop=k == KC - 1)
                        x.then_inc(cv_ps, 1)

            def z(j, out, col, width, done):
                for k in range(KC):
                    x = pe.matmul(out, xTs[j][:, k, :], wtok[:, k, col:col + width], start=k == 0, stop=k == KC - 1)
                x.then_inc(done, 1)

            def z_lr(n, j):
                pe.wait_ge(xTs_rdy, n + 1)
                z(j, bk["lr"][:, 0:LR], 2 * QW + 2 * VW, LR, lr_ps)

            def z_qk(j):
                z(j, bk["qk"], 0, 2 * QW, qk_ps)

            def z_v(n, j):
                if late(n, 1):
                    pe.wait_ge(v_rdy, n)
                z(j, bk["v"], 2 * QW, VW, v_ps)

            def z_og(n, j):
                if late(n, 1):
                    pe.wait_ge(gog_rdy, n)
                z(j, bk["og"], 2 * QW + VW, VW, og_ps)

            def lr_T(n):
                pe.wait_ge(lr_rdy, n + 1)
                pe.transpose(bk["lr"][0:LR, LR:LR + P], lr_sb[:], ident).then_inc(lrT_ps, 1)

            def log_gate(n):
                pe.wait_ge(lrT_rdy, n + 1)
                pe.matmul(bk["lr"][:, 144:400], lrT[:], wf[:], start=True, stop=True).then_inc(lap_ps, 1)

            def cumulate(n):
                samples = isinstance(n, int) and n == NT - 1
                pe.wait_ge(la_rdy, n + 1)
                pe.matmul(bk["lr"][:, 144:400], C["tris" if samples else "tric"], la[:], start=True, stop=True)
                m = C["seqsum" if samples else "halves"]
                w = NB if samples else 2
                for hd in range(H):
                    x = pe.matmul(bk["lr"][0:DK, 400 + w * hd:400 + w * (hd + 1)], la[:, hd * DK:(hd + 1) * DK], m,
                                  start=True, stop=True)
                x.then_inc(b_ps, 1)

            def turn(n):
                pe.wait_ge(qk_rdy, n + 1)
                if late(n, 1):
                    pe.wait_ge(S_rdy, n)
                pe.matmul(bk["qT"][0:DK, 0:P], qk[:, 0:DK], ident, start=True, stop=True)
                for hd in range(1, H):
                    pe.transpose(bk["qT"][0:DK, hd * P:(hd + 1) * P], qk[:, hd * DK:(hd + 1) * DK], ident)
                for hd in range(H):
                    x = pe.transpose(bk["kT"][0:DK, hd * P:(hd + 1) * P], qk[:, QW + hd * DK:QW + (hd + 1) * DK], ident)
                x.then_inc(qkT_ps, 1)

            def scores(n):
                pe.wait_ge(qT_rdy, n + 1)
                pe.wait_ge(kT_rdy, n + 1)
                for hd in range(H):
                    x = pe.matmul(bk["sc"][:, hd * P:(hd + 1) * P], qkT[:, H + hd, :], qkT[:, hd, :], start=True, stop=True)
                x.then_inc(sc_ps, 1)

            def outputs(n, j):
                pe.wait_ge(PT_rdy, n + 1)
                pe.wait_ge(Sm_rdy, 2 * n + 1)
                pe.wait_ge(v_rdy, n + 1)
                if late(n, 1):
                    pe.wait_ge(o_rdy, n)
                for hd in range(H):
                    out = bk["o"][:, hd * DV:(hd + 1) * DV]
                    pe.matmul(out, qkT[:, hd, :], Smid[:, hd, :], start=True, stop=False)
                    x = pe.matmul(out, PT[:, hd, :], v_sb[j][:, hd * DV:(hd + 1) * DV], start=False, stop=True)
                x.then_inc(o_ps, 1)
                for hd in range(H):
                    x = pe.matmul(bk["qT"][0:DK, hd * DV:(hd + 1) * DV], qk[:, QW + hd * DK:QW + (hd + 1) * DK],
                                  v_sb[j][:, hd * DV:(hd + 1) * DV], start=True, stop=True)
                x.then_inc(U_ps, 1)

            def gla(n, j):
                turn(n)
                z_lr(n + 1, 1 - j)
                z_qk(1 - j)
                lr_T(n + 1)
                scores(n)
                log_gate(n + 1)
                z_v(n + 1, 1 - j)
                cumulate(n + 1)
                outputs(n, j)
                z_og(n + 1, 1 - j)

            pe.wait_ge(cv_sb, 6 * CC)
            pe.wait_ge(wtok_in, 16)
            pe.wait_ge(c_in, 16 * (len(SMALL) + 1))
            z_lr(0, 0)
            z_qk(0)
            lr_T(0)
            log_gate(0)
            z_v(0, 0)
            cumulate(0)
            z_og(0, 0)
            gla(0, 0)
            with pe.Fori(0, 3) as i:
                gla(2 * i + 1, 1)
                gla(2 * i + 2, 0)
            gla(NT - 2, 1)
            n = NT - 1
            turn(n)
            scores(n)
            pe.wait_ge(gog_rdy, NT)
            pe.wait_ge(v_rdy, NT)
            pe.wait_ge(E_rdy, NT)
            pe.wait_ge(conv, 2 * K * CC)
            for part, src in enumerate([cT, csq]):
                for c in range(CC):
                    for b in range(NBLK):
                        if part and b == 0:
                            pe.wait_ge(csq_rdy, c + 1)
                        x = pe.matmul(psum[:, 3 * part + b, 0:BLK], C["ones"], src[:, c, b * BLK:(b + 1) * BLK],
                                      start=c == 0, stop=c == CC - 1)
            x.then_inc(st_ps, 1)
            pe.wait_ge(PT_rdy, n + 1)
            pe.wait_ge(o_rdy, n)
            pe.wait_ge(smp, 1)
            pe.wait_ge(s0_in, 16)
            for hd in range(H):
                out = bk["o"][0:NS, hd * DV:(hd + 1) * DV]
                for b in range(NB):
                    pe.matmul(out, qm[:, hd, b, :], s0[:, b, hd, :], start=b == 0, stop=False)
                x = pe.matmul(out, PT[:, hd, 0:NS], v_sb[0][:, hd * DV:(hd + 1) * DV], start=False, stop=True)
            x.then_inc(o_ps, 1)
            pe.wait_ge(ln_v, 3)
            for b in range(NB):
                if b >= 6:
                    pe.wait_ge(SU_add, b - 5)
                for hd in range(H):
                    x = pe.matmul(psum[0:DK, b % 6, hd * DV:(hd + 1) * DV], km[:, b, hd * DK:(hd + 1) * DK],
                                  v_sb[0][:, hd * DV:(hd + 1) * DV], start=True, stop=True)
                x.then_inc(SU_ps, 1)

            def turn_o(n, j):
                pe.wait_ge(og_rdy, n + 1)
                if late(n, 1):
                    pe.wait_ge(catT_o, n)
                for hd in range(H):
                    x = pe.transpose(psum[:, 4, hd * P:(hd + 1) * P], og[j][:, hd * DV:(hd + 1) * DV], ident)
                x.then_inc(oT_ps, 1)

            def project(n, j, half):
                pe.wait_ge(catT_o, n + 1)
                pe.wait_ge(catT_c, n + 1)
                if late(n, 2):
                    pe.wait_ge(h_rdy, n - 1)
                for k in range(KC):
                    x = pe.matmul(psum[:, 2 * j + half, :], catT[j][:, k, :], wout[:, k, half * 512:(half + 1) * 512],
                                  start=k == 0, stop=k == KC - 1)
                x.then_inc(w_ps, 1)

            def turn_xn2(n, j):
                pe.wait_ge(xn2_rdy, n + 1)
                for k in range(KC):
                    x = pe.transpose(psum[:, 5 + k // 4, (k % 4) * P:(k % 4 + 1) * P], xn2[j][:, k * P:(k + 1) * P], ident)
                x.then_inc(xn2T_ps, 1)

            def route(n, j):
                pe.wait_ge(xn2T_a, n + 1)
                pe.wait_ge(xn2T_v, n + 1)
                if late(n, 1):
                    pe.wait_ge(lg_rdy, n)
                for k in range(KC):
                    x = pe.matmul(psum[:, 7, 0:G + NE], xn2T[j][:, k, :], wr[:, k, :], start=k == 0, stop=k == KC - 1)
                x.then_inc(lg_ps, 1)

            def mix(n, j):
                project(n, j, 0)
                if late(n, 1):
                    turn_xn2(n - 1, 1 - j)
                if not (isinstance(n, int) and n == NT - 1):
                    turn_o(n + 1, 1 - j)
                project(n, j, 1)
                if late(n, 1):
                    route(n - 1, 1 - j)

            pe.wait_ge(SU_add, NB)
            pe.wait_ge(wout_in, 16)
            turn_o(0, 0)
            tiles(pe, mix)
            turn_xn2(NT - 1, 0)
            route(NT - 1, 0)

            pe.wait_ge(M_rdy, 1)
            pe.matmul(psum[:, 0, 0:NT * NE], C["upper"], Msum.rearrange("p a b -> p (a b)"), start=True, stop=True)
            pe.matmul(psum[:, 1, 0:NT * NE], C["ones"], Msum.rearrange("p a b -> p (a b)"), start=True, stop=True).then_inc(rk_ps, 1)
            for m in range(2):
                pe.wait_ge(oh_rdy, m + 1)
                for n in range(m * NT, (m + 1) * NT):
                    x = pe.matmul(psum[:, 2, 0:NTILE], ohr[:, n, :], oht[:, n, :], start=n == 0, stop=n == 2 * NT - 1)
            x.then_inc(ids_ps, 1)

            def turn_rows(src, done):
                for k in range(KC):
                    x = pe.transpose(psum[:, k // 4, (k % 4) * P:(k % 4 + 1) * P], src[:, k * P:(k + 1) * P], ident)
                x.then_inc(done, 1)

            def turn_xg(t, sl, landed=None):
                pe.wait_ge(xg_in[sl], turn_of(t, sl) * 16 + 16 if landed is None else landed)
                turn_rows(xg[sl], xgT_ps)

            def mm_gate_up(sl, done):
                for k in range(KC):
                    x = pe.matmul(psum[:, 2 + sl, :], xgT[sl][:, k, :], wgu[sl][:, k, :], start=k == 0, stop=k == KC - 1)
                x.then_inc(done, 1)

            def mm_turn_h(done):
                for k in range(FC):
                    x = pe.transpose(psum[:, 5, k * P:(k + 1) * P], hg[:, k * P:(k + 1) * P], ident)
                x.then_inc(done, 1)

            def mm_down(sl, done):
                for half in range(2):
                    for k in range(FC):
                        x = pe.matmul(psum[:, 6 + half, :], hT[:, k, :], wdn[sl][:, k, half * 512:(half + 1) * 512],
                                      start=k == 0, stop=k == FC - 1)
                x.then_inc(done, 1)

            def down(t, sl, landed=None):
                pe.wait_ge(hT_rdy, t + 1)
                pe.wait_ge(dn_in[sl], turn_of(t, sl) * 16 + 16 if landed is None else landed)
                if late(t, 1):
                    pe.wait_ge(y_a, t)
                    pe.wait_ge(y_v, t)
                mm_down(sl, y_ps)

            def expert(t, sl):
                pe.wait_ge(xgT_a, t + 1)
                pe.wait_ge(xgT_v, t + 1)
                pe.wait_ge(gu_in[sl], turn_of(t, sl) * 16 + 16)
                mm_gate_up(sl, gu_ps)
                if isinstance(t, int) and t == NE - 1:
                    with pe.If(count > 0):
                        turn_xg(NE, 2, extra_turn(0, 2))
                else:
                    turn_xg(t + 1, (sl + 1) % 3)
                if late(t, 1):
                    down(t - 1, (sl - 1) % 3)
                pe.wait_ge(hg_rdy, t + 1)
                mm_turn_h(hT_ps)

            pe.wait_ge(pos_rdy, 1)
            count = pe.value_load(plan[0:1, EXTRA + 2:EXTRA + 3], min_val=0, max_val=EXTRA)
            turn_xg(0, 0)
            experts(pe, expert)
            with pe.If(count == 0):
                down(NE - 1, (NE - 1) % 3)

            def expert_extra(t, sl):
                pe.wait_ge(xgT_a, t + NE + 1)
                pe.wait_ge(xgT_v, t + NE + 1)
                pe.wait_ge(gu_in[sl], extra_turn(t, sl))
                mm_gate_up(sl, gu_ps)
                with pe.If(count > t + 1):
                    turn_xg(t + NE + 1, 3 - sl, extra_turn(t + 1, 3 - sl))
                down(t + NE - 1, 3 - sl, extra_turn(t - 1, 3 - sl))
                pe.wait_ge(hg_rdy, t + NE + 1)
                mm_turn_h(hT_ps)
                with pe.If(count == t + 1):
                    down(t + NE, sl, extra_turn(t, sl))

            extra(pe, count, expert_extra)
            pe.nop().then_inc(moe_done, 1)

            def turn_x3(n, j):
                pe.wait_ge(xn3_rdy, n + 1)
                if late(n, 1):
                    pe.wait_ge(x3T_a, n)
                    pe.wait_ge(x3T_v, n)
                turn_rows(xn3[j], x3T_ps)

            def project_p(n, j):
                pe.wait_ge(pT_in[j], 8 * (n - j) + 16)
                if late(n, 1):
                    pe.wait_ge(mix_rdy, 2 * n - 1)
                for half in range(2):
                    for k in range(PC):
                        x = pe.matmul(psum[:, 4 + half, :], pT[j][:, k, :], wproj[:, k, half * 512:(half + 1) * 512],
                                      start=k == 0, stop=k == PC - 1)
                x.then_inc(pr_ps, 1)

            def gate_half(n, j, half):
                pe.wait_ge(x3T_a, n + 1)
                pe.wait_ge(x3T_v, n + 1)
                if late(n, 2):
                    pe.wait_ge(sg_rdy, n - 1)
                for k in range(KC):
                    x = pe.matmul(psum[:, 2 + 4 * j + half, :], x3T[j][:, k, :], wple[k][:, half * 512:(half + 1) * 512],
                                  start=k == 0, stop=k == KC - 1)
                x.then_inc(gt_ps, 1)

            def embed(n, j):
                gate_half(n, j, 0)
                project_p(n, j)
                if not (isinstance(n, int) and n == NT - 1):
                    turn_x3(n + 1, 1 - j)
                gate_half(n, j, 1)

            pe.wait_ge(pw_in, 48)
            pe.wait_ge(wple_in, 16 * KC)
            turn_x3(0, 0)
            embeds(pe, embed)


def layout(x_prompt, x_sample, state_gla, state_conv, p_prompt, p_sample, g_mix, w_in, w_forget_up, b_forget, g_gla_out,
           w_conv, b_conv, g_conv_ln, b_conv_ln, w_out, g_ffn, w_grp_router, b_grp_router, w_exp_router, b_exp_router,
           w_exp_gate, w_exp_up, w_exp_down, g_ple, w_ple_gate, w_ple_proj, g_final):
    cat = np.concatenate

    def chunked(w):
        return np.swapaxes(w.reshape(-1, P, *w.shape[1:]), 0, 1)

    w = w_in[0]
    pad = NT * P - SEQ - NS
    w_cv = w[:, TW:].reshape(KC, P, 2, CC, P).transpose(3, 1, 0, 2, 4).reshape(CC, P, KC, 2 * P)
    return dict(
        consts=constants(),
        x=cat([x_prompt[0], x_sample.reshape(NS, D), np.zeros((pad, D), np.float32)]),
        w_tok=chunked(w[:, :TW]), w_cv=w_cv,
        state_conv=state_conv[0].transpose(2, 0, 1).reshape(CC, P, NB, HIST).transpose(1, 0, 2, 3),
        state_gla=state_gla[0].transpose(2, 0, 1, 3),
        w_conv=chunked(w_conv[0].T), conv_vecs=np.stack([v[0].reshape(CC, P).T for v in (b_conv, g_conv_ln, b_conv_ln)], 1),
        g_gla_out=g_gla_out[0][:, None], w_forget=cat([w_forget_up[0], b_forget]), w_out=chunked(w_out[0]),
        w_router=chunked(cat([w_grp_router[0], w_exp_router[0].transpose(1, 0, 2).reshape(D, NE)], 1)),
        b_router=cat([b_grp_router[0], b_exp_router[0].reshape(NE)])[None],
        w_gu=cat([w_exp_gate[0], w_exp_up[0]], -1).reshape(NE, KC, P, 2 * FF).transpose(0, 2, 1, 3),
        w_dn=w_exp_down[0].reshape(NE, FC, P, D).transpose(0, 2, 1, 3),
        w_ple=chunked(w_ple_gate[0]), w_proj=chunked(w_ple_proj[0]),
        pT=cat([p_prompt[0, 0], p_sample[0].reshape(NS, PLE), np.zeros((pad, PLE), np.float32)])
        .reshape(NT, P, PC, P).transpose(0, 3, 2, 1),
        g_mix=g_mix, g_ffn=g_ffn, g_ple=g_ple, g_final=g_final[None],
    )


OUTS = dict(y=(TOK, D), gla_prompt=(DK, H, DV), gla_sample=(DK, NB, H, DV), conv_prompt=(P, CC, HIST),
            conv_sample=(P, CC, NB, HIST))
SCRATCH = dict(xn2=((TOK, D), F32), yrows=((NTILE * P, D), F32))


def kernel(**inputs):
    import concourse.bacc as bacc
    from concourse.bass_utils import run_bass_kernel_spmd

    nc = bacc.Bacc("TRN2", target_bir_lowering=False, num_devices=1)
    arrays, ins, outs = {}, {}, {}
    for name, v in layout(**{k: np.asarray(x) for k, x in inputs.items()}).items():
        arrays["in_" + name] = v = np.ascontiguousarray(v)
        ins[name] = nc.dram_tensor("in_" + name, v.shape, mybir.dt.from_np(v.dtype), kind="ExternalInput").ap()
    for name, (shape, dt) in SCRATCH.items():
        ins[name] = nc.dram_tensor(name, shape, dt, kind="Internal").ap()
    for name, shape in OUTS.items():
        outs[name] = nc.dram_tensor("out_" + name, shape, F32, kind="ExternalOutput").ap()
    bass_decoder_step(nc, ins, outs)
    r = run_bass_kernel_spmd(nc, [arrays], core_ids=[0]).results[0]
    y = r["out_y"]
    return (y[None, :SEQ], y[SEQ:SEQ + NS].reshape(NB, TB, D),
            r["out_gla_prompt"].transpose(1, 0, 2)[None, None],
            r["out_gla_sample"].transpose(1, 2, 0, 3)[None],
            r["out_conv_prompt"].transpose(2, 1, 0).reshape(1, 1, HIST, CW),
            r["out_conv_sample"].transpose(2, 3, 1, 0).reshape(1, NB, HIST, CW))
```

```python
from contextlib import ExitStack

import concourse.bass as bass
import numpy as np
from concourse import mybir
from concourse.alu_op_type import AluOpType as ALU

F32 = mybir.dt.float32
F16 = mybir.dt.float16
I32 = mybir.dt.int32
ACT = mybir.ActivationFunctionType
AX = mybir.AxisListType.X

P = 128
D = 1024
KC = D // P
SEQ = 1024
NB, TB = 8, 8
NS = NB * TB
NT = SEQ // P + 1
TOK = NT * P
H, DK, DV = 4, 64, 128
QW, VW = H * DK, H * DV
LR = 16
TW = 2 * QW + 2 * VW + LR
CW = 512
CC = CW // P
K = 31
HIST = K - 1
BLK = 384
NBLK = TOK // BLK
G, E, FF = 4, 8, 256
NE = G * E
FC = FF // P
PLE = 256
PC = PLE // P
EPS = 1e-6
TAU = 16.0
MID = P // 2
BIG = 1e30
EXTRA = (2 * (SEQ + NS)) // (P + 1)
NTILE = NE + EXTRA

CONSTS = [("ident", P), ("tric", P), ("tris", P), ("cmask", P), ("cmasks", P), ("upper", P), ("ones", P),
          ("halves", 2), ("seqsum", NB), ("seqone", NB), ("desc8", E), ("desc4", G), ("eidx", NE),
          ("steps", E), ("tidx", EXTRA), ("count", P), ("token", NT),
          ("inner", NE * NT)]
CAT, _at = {}, 0
for _name, _w in CONSTS:
    CAT[_name] = (_at, _w)
    _at += _w
CONST_W = _at


def constants():
    s, t = np.arange(P)[:, None], np.arange(P)[None, :]
    c = np.zeros((P, CONST_W), np.float32)

    def put(name, v):
        a, w = CAT[name]
        c[:, a:a + w] = v

    same = (s // TB == t // TB)
    put("ident", s == t)
    put("tric", ((s <= t) * 1.0 - (s < MID) * 1.0) / TAU)
    put("tris", (same & (s <= t)) / TAU)
    put("cmask", s <= t)
    put("cmasks", same & (s <= t))
    put("upper", s < t)
    put("ones", 1.0)
    put("halves", np.concatenate([s < MID, s >= MID], 1) / TAU)
    b = np.arange(NB)[None, :]
    put("seqsum", (s // TB == b) / TAU)
    put("seqone", s // TB == b)
    put("desc8", E - np.arange(E)[None, :])
    put("desc4", G - np.arange(G)[None, :])
    put("eidx", np.arange(NE)[None, :])
    put("steps", P * (1 + np.arange(E))[None, :])
    put("tidx", np.arange(EXTRA)[None, :])
    put("count", t)
    put("inner", (np.arange(NE * NT) % NT != 0)[None, :])
    token = np.arange(NT)[None, :] * P + s
    put("token", token * (token < SEQ + NS))
    return c


def experts(eng, body):
    for t in range(4):
        body(t, t % 3)
    with eng.Fori(1, (NE - 2) // 3) as i:
        for k in range(1, 4):
            body(3 * i + k, k % 3)
    body(NE - 1, (NE - 1) % 3)


def extra(eng, count, body):
    with eng.Fori(0, EXTRA // 4) as i:
        with eng.If(count > 4 * i):
            for j in range(4):
                with eng.If(count > 4 * i + j):
                    body(4 * i + j, 2 - j % 2)


def embeds(eng, body):
    body(0, 0)
    body(1, 1)
    with eng.Fori(1, (NT - 3) // 2) as i:
        body(2 * i, 0)
        body(2 * i + 1, 1)
    for n in range(NT - 3, NT):
        body(n, n % 2)


def turn_of(t, s):
    return t // 3 if isinstance(t, int) else (t - s) // 3


def extra_turn(t, s):
    return 16 * ((NE + 2 - s) // 3) + 8 * (t - (2 - s)) + 16


def hold(eng, passed):
    eng.sem_inc(passed, 1)


def late(n, k):
    return not isinstance(n, int) or n >= k


def tiles(eng, body):
    body(0, 0)
    body(1, 1)
    with eng.Fori(1, (NT - 1) // 2) as i:
        body(2 * i, 0)
        body(2 * i + 1, 1)
    body(NT - 1, 0)


def bass_decoder_step(nc, a, o):
    with ExitStack() as ctx:
        arena = ctx.enter_context(nc.sbuf_tensor("arena", [P, 40888], F32))
        psum = ctx.enter_context(nc.psum_tensor("psum", [P, 8, 512], F32))

        def at(start, *shape):
            n = int(np.prod(shape))
            v = arena[:, start:start + n]
            if len(shape) == 2:
                v = v.rearrange("p (a b) -> p a b", b=shape[1])
            elif len(shape) == 3:
                v = v.rearrange("p (a b c) -> p a b c", b=shape[1], c=shape[2])
            return v

        def halves(start, *shape):
            n = int(np.prod(shape)) // 2
            return [at(start + i * n, n).bitcast(F16).rearrange("p (a b) -> p a b", b=shape[1]) for i in range(2)]

        def sb(name, *shape, dt=F32, parts=P):
            return ctx.enter_context(nc.sbuf_tensor(name, [parts, *shape], dt))

        def sem(name):
            return ctx.enter_context(nc.semaphore(name))

        R1, R2, R3, R4, R5 = 0, 9216, 21632, 30848, 36280
        xnT = halves(R1, KC, TOK)
        wtok = halves(R2, KC, TW)
        wcv_raw = at(R3, KC, 2 * P)
        wcv = [halves(R3 + 2048 * (j + 1), KC, 2 * P) for j in range(2)]
        a_sb = at(R3 + 6144, TOK)
        sg_sb = at(R3 + 6144 + TOK, TOK)
        xt = at(R2, NT, D)
        sqj = [at(R5 + 1024 * j, D) for j in range(2)]
        xs = [at(R5 + 2048 + 1024 * j, D) for j in range(2)]
        UW = HIST + SEQ
        SW = HIST + TB
        u = at(R4, CC, UW)
        us = at(R4 + CC * UW, CC, NB * SW).rearrange("p c (b t) -> p c b t", t=SW)
        cT = at(R5, CC, TOK)
        oraw = at(R3, NT, VW)
        gog = at(R3 + NT * VW, NT, VW)
        s0 = at(R2 + 4096, NB, H * DV)[0:DK].rearrange("p b (h d) -> p b h d", d=DV)
        qm = at(R2, H, NB, NS)[0:DK]
        km = at(R2 + 2048, NB, QW)
        csq = at(R4, CC, TOK)
        h = at(R2, NT, D)
        mean = at(R2 + NT * D, TOK)
        rstdb = at(R2 + NT * D + TOK, TOK)
        wout = halves(R1, KC, D)
        wo_raw = [at(R1 + KC * D, D), at(R2 + KC * D, D)]
        catT = [halves(R4 + 1024 * j, KC, P) for j in range(2)]
        xn2T = [at(R4 + 2048 + 1024 * j, KC, P) for j in range(2)]
        xn2 = [at(R2 + NT * D + 1024 * j, D) for j in range(2)]

        RT = R2 + NT * D
        M12 = at(RT, 2, NT, NE)
        Msum = at(RT + 576, NT * NE // 2).bitcast(F16)
        rank = at(RT + 864, NE * NT)
        upto = at(RT + 1152, NE * NT)
        prod = at(RT + 1472, 2 * NT, NE)
        cmpe = at(RT + 2048, NE, E)
        cmpt = at(R4 + 7424, EXTRA, NE)
        RS = R1 + KC * D
        gd = at(RS, NT, G)
        gsc = at(RS + 36, NT, G)
        ohg = at(RS + 72, NT, G)
        sel = at(RS + 108, NT, E)
        esc = at(RS + 180, NT, E)
        oh = [at(RS + 252 + 72 * m, NT, E) for m in range(2)]
        cmpr = at(RS + 396, 2 * NT, E)
        one = {n: at(RS + 540 + 9 * i, NT)
               for i, n in enumerate(["gmax", "gm", "gsum", "gw", "v1", "m1", "v2", "m2", "dv", "ev"])}
        two = {n: at(RS + 640 + 18 * i, 2 * NT) for i, n in enumerate(["rank", "exp", "ovb", "q", "isq", "t", "r", "fy"])}
        nx = at(RS + 810, NE)
        inc = at(RS + 842, NE)
        ovb = at(RS + 874, NE)
        et = at(RS + 906, EXTRA)
        ohr = at(R3 + 6144, NT * P).bitcast(F16).rearrange("p (a b) -> p a b", b=P)
        oht = at(R4 + 6144, NT * NTILE).bitcast(F16).rearrange("p (a b) -> p a b", b=NTILE)
        WAT = [R1, R3, R4]
        wgu = [at(w, KC, 2 * FF) for w in WAT]
        wdn = [at(w + KC * 2 * FF, FC, D) for w in WAT]
        xg = [at(RT + D * s, D) for s in range(3)]
        xgT = [at(R3 + 6144 + D * s, KC, P) for s in range(3)]
        yt = [at(R1 + 6144 + D * s, D) for s in range(3)]
        sil = [at(R4 + 6144 + FF * s, FF) for s in range(3)]
        hg = at(R4 + 6912, FF)
        hT = at(R4 + 7168, FC, P)
        wple = [at(R1 + D * k, D) if k < 6 else at(R4 + 7992 + D * (k - 6), D) for k in range(KC)]
        yg = [[at(R3 + 2048 * j + D * m, D) for m in range(2)] for j in range(2)]
        xn3 = [at(R3 + 4096 + D * j, D) for j in range(2)]
        x3T = [halves(R3 + 6144 + D * j, KC, P) for j in range(2)]
        wgate = [halves(w, 1, D) for w in [R4 + 4608, R4 + 5632, R4 + 6656, R1 + 6144, R1 + 7168, R1 + 8192, R1, R1 + D]]
        yo = [at(RT + D * j, D) for j in range(2)]
        wproj = at(R4, PC, D)
        mixd = [at(R4 + 2560 + D * j, D) for j in range(2)]

        cst = sb("cst", CONST_W)
        C = {n: cst[:, s:s + w] for n, (s, w) in CAT.items()}
        side = [sb(f"side{j}", KC, P) for j in range(2)]
        g1 = sb("g1", D)
        TH = TW // 2
        wt_raw = [side[j][:].rearrange("p a b -> p (a b)")[:, 0:TH] for j in range(2)]
        wo_raw += [side[j][:].rearrange("p a b -> p (a b)") for j in range(2)]
        sprod = side[0][:, 0:CC * NB * TB // P, :].rearrange("p a b -> p (a b)").rearrange("p (c b t) -> p c b t", c=CC, t=TB)
        gfin = side[0][:].rearrange("p a b -> p (a b)")
        pT = [side[1][:, PC * j:PC * (j + 1), :] for j in range(2)]
        ssq = sb("ssq", 2)
        std = sb("std", 2)
        rst = sb("rst", 2)
        wc = sb("wc", CC, K)
        cvec = sb("cvec", 3, CC)
        ggo = sb("ggo", 1)
        gghalf = sb("gghalf", 1)
        wf = sb("wf", QW, parts=LR + 1)
        lr_sb = sb("lr_sb", LR)
        lrT = sb("lrT", P, parts=LR + 1)
        absx = sb("absx", QW)
        la = sb("la", QW)
        E1 = sb("E1", QW)
        E2 = sb("E2", QW)
        EL = [sb(f"EL{j}", H, 2, parts=DK) for j in range(2)]
        ELs = sb("ELs", H, NB, parts=DK)
        v_sb = [sb(f"v{j}", VW) for j in range(2)]
        th = sb("th", VW)
        qk = sb("qk", 2 * QW)
        qkT = sb("qkT", 2 * H, P, parts=DK)
        PT = sb("PT", H, P)
        St = sb("St", H, DV, parts=DK)
        Smid = sb("Smid", H, DV, parts=DK)
        Slast = sb("Slast", H, DV, parts=DK)
        eps = sb("eps", 1)
        osq = sb("osq", 2, H)
        ostd = sb("ostd", 2, H)
        orst = sb("orst", 2, H)
        og = [at(RT + 2304, VW), v_sb[1][:]]
        wr = sb("wr", KC, G + NE)
        upper16 = sb("upper16", P, dt=F16)
        ones16 = sb("ones16", P, dt=F16)
        brb = sb("brb", G + NE)
        logits = sb("logits", NT, G + NE)
        ids = sb("ids", NTILE, dt=I32)
        idx = [sb(f"idx{s}", 1, dt=I32) for s in range(3)]
        idy = [[sb(f"idy{j}{m}", 1, dt=I32) for m in range(2)] for j in range(2)]
        posY = sb("posY", 2 * NT, dt=I32)
        w12 = sb("w12", 2, NT)
        plan = sb("plan", EXTRA + 3, dt=I32)

        c_in = sem("c_in")
        g1_in = sem("g1_in")
        x_in = [sem(f"x_in{j}") for j in range(2)]
        ssq_rdy = sem("ssq_rdy")
        std_rdy = sem("std_rdy")
        rst_rdy = sem("rst_rdy")
        xs_rdy = sem("xs_rdy")
        xT_ps = sem("xT_ps")
        xnT_a = sem("xnT_a")
        xnT_v = sem("xnT_v")
        wcv_in = sem("wcv_in")
        wcv_hi = sem("wcv_hi")
        wcv_lo = sem("wcv_lo")
        wt_in = [sem(f"wt_in{j}") for j in range(2)]
        wt_hi = sem("wt_hi")
        wt_lo = sem("wt_lo")
        cv_ps = sem("cv_ps")
        cv_sb = sem("cv_sb")
        u_rdy = sem("u_rdy")
        zero = sem("zero")
        conv = sem("conv")
        sconv = sem("sconv")
        hist_in = sem("hist_in")
        cst_out = sem("cst_out")
        lr_ps = sem("lr_ps")
        lr_rdy = sem("lr_rdy")
        lrT_ps = sem("lrT_ps")
        lrT_rdy = sem("lrT_rdy")
        lap_ps = sem("lap_ps")
        absx_rdy = sem("absx_rdy")
        la_rdy = sem("la_rdy")
        b_ps = sem("b_ps")
        E_rdy = sem("E_rdy")
        qk_ps = sem("qk_ps")
        v_ps = sem("v_ps")
        og_ps = sem("og_ps")
        v_rdy = sem("v_rdy")
        th_rdy = sem("th_rdy")
        gog_rdy = sem("gog_rdy")
        qk_rdy = sem("qk_rdy")
        qkT_ps = sem("qkT_ps")
        qT_rdy = sem("qT_rdy")
        kT_rdy = sem("kT_rdy")
        sc_ps = sem("sc_ps")
        PT_rdy = sem("PT_rdy")
        o_ps = sem("o_ps")
        o_rdy = sem("o_rdy")
        U_ps = sem("U_ps")
        S_rdy = sem("S_rdy")
        Sm_rdy = sem("Sm_rdy")
        s0_in = sem("s0_in")
        smp = sem("smp")
        SU_ps = sem("SU_ps")
        SU_add = sem("SU_add")
        SU_out = sem("SU_out")
        csq_rdy = sem("csq_rdy")
        st_ps = sem("st_ps")
        ln_v = sem("ln_v")
        ln_std = sem("ln_std")
        ln_x = sem("ln_x")
        ln_sub = sem("ln_sub")
        ln_psub = sem("ln_psub")
        cT_rdy = sem("cT_rdy")
        wo_in = [sem(f"wo_in{j}") for j in range(2)]
        wl_hi = sem("wl_hi")
        wl_lo = sem("wl_lo")
        g2_in = sem("g2_in")
        osq_rdy = sem("osq_rdy")
        ostd_rdy = sem("ostd_rdy")
        orst_rdy = sem("orst_rdy")
        og_rdy = sem("og_rdy")
        oT_ps = sem("oT_ps")
        catT_o = sem("catT_o")
        catT_l = sem("catT_l")
        catT_c = sem("catT_c")
        w_ps = sem("w_ps")
        x2_in = [sem(f"x2_in{j}") for j in range(2)]
        h_rdy = sem("h_rdy")
        xn2_rdy = sem("xn2_rdy")
        xn2_out = [sem(f"xn2_out{j}") for j in range(2)]
        xn2T_ps = sem("xn2T_ps")
        xn2T_a = sem("xn2T_a")
        xn2T_v = sem("xn2T_v")
        lg_ps = sem("lg_ps")
        lg_rdy = sem("lg_rdy")
        out_st = sem("out_st")
        rt = sem("rt")
        ge_rdy = sem("ge_rdy")
        gd_rdy = sem("gd_rdy")
        ev_rdy = sem("ev_rdy")
        dv_rdy = sem("dv_rdy")
        M_rdy = sem("M_rdy")
        rk_ps = sem("rk_ps")
        pos_rdy = sem("pos_rdy")
        oh_rdy = sem("oh_rdy")
        ids_ps = sem("ids_ps")
        ids_rdy = sem("ids_rdy")
        idx_rdy = sem("idx_rdy")
        passed = sem("passed")
        xg_in = [sem(f"xg_in{s}") for s in range(3)]
        gu_in = [sem(f"gu_in{s}") for s in range(3)]
        dn_in = [sem(f"dn_in{s}") for s in range(3)]
        xgT_ps = sem("xgT_ps")
        xgT_a = sem("xgT_a")
        xgT_v = sem("xgT_v")
        gu_ps = sem("gu_ps")
        sil_rdy = sem("sil_rdy")
        hg_rdy = sem("hg_rdy")
        hT_ps = sem("hT_ps")
        hT_rdy = sem("hT_rdy")
        y_ps = sem("y_ps")
        y_a = sem("y_a")
        y_v = sem("y_v")
        y_out = [sem(f"y_out{s}") for s in range(3)]
        y_all = sem("y_all")
        y_zero = sem("y_zero")
        moe_done = sem("moe_done")
        idy_rdy = sem("idy_rdy")
        yg_in = [[sem(f"yg_in{j}{m}") for m in range(2)] for j in range(2)]
        wple_in = sem("wple_in")
        pw_in = sem("pw_in")
        pT_in = [sem(f"pT_in{j}") for j in range(2)]
        add_rdy = sem("add_rdy")
        std3_rdy = sem("std3_rdy")
        rst3_rdy = sem("rst3_rdy")
        xn3_rdy = sem("xn3_rdy")
        x3T_ps = sem("x3T_ps")
        x3T_a = sem("x3T_a")
        x3T_v = sem("x3T_v")
        pr_ps = sem("pr_ps")
        gt_ps = sem("gt_ps")
        sg_rdy = sem("sg_rdy")
        mix_rdy = sem("mix_rdy")
        ssq4_rdy = sem("ssq4_rdy")
        std4_rdy = sem("std4_rdy")
        rst4_rdy = sem("rst4_rdy")
        y_rdy = sem("y_rdy")
        fin_out = [sem(f"fin_out{j}") for j in range(2)]

        SMALL = [(wc[:], "w_conv"), (cvec[:], "conv_vecs"), (ggo[:], "g_gla_out"), (wf[:], "w_forget"),
                 (wr[:], "w_router")]
        ZB = dict(qk=0, v=1, og=2, lr=3, kT=4, qT=5, sc=6, o=7)
        bk = {n: psum[:, b, :] for n, b in ZB.items()}

        def rows(t, n):
            return t[bass.ds(n * P, P), :]

        def w_pieces(eng, c, body):
            first, last = [(0, 3), (3, 6), (6, KC), (KC, KC)][c]
            if c == 0:
                body(0, 0)
                body(0, 1)
                first = 1
            if first < last:
                with eng.Fori(first, last) as k:
                    body(k, 0)
                    body(k, 1)

        block = ctx.enter_context(nc.Block())

        @block.sync
        def _(sp):
            def load_x(n, j):
                if late(n, 2):
                    sp.wait_ge(x_in[j], 8 * (n - j))
                sp.dma_start(xt[:, bass.ds(n, 1), :].rearrange("p a b -> p (a b)"), rows(a["x"], n)).then_inc(x_in[j], 16)

            load_x(0, 0)
            sp.dma_start(g1[:], a["g_mix"].to_broadcast([P, D])).then_inc(g1_in, 16)
            sp.dma_start(cst[:], a["consts"]).then_inc(g1_in, 16)
            load_x(1, 1)
            with sp.Fori(1, (NT - 1) // 2) as i:
                load_x(2 * i, 0)
                load_x(2 * i + 1, 1)
            load_x(NT - 1, 0)
            def load_wt(k, half):
                if late(k, 1):
                    sp.wait_ge(wt_lo, 2 * k + half - 1)
                sp.dma_start(wt_raw[half], a["w_tok"][:, bass.ds(k, 1), half * TH:(half + 1) * TH]
                             .rearrange("p a f -> p (a f)")).then_inc(wt_in[half], 16)

            sp.dma_start(wcv_raw, a["w_cv"][0]).then_inc(wcv_in, 16)
            for dst, name in SMALL:
                sp.dma_start(dst, a[name]).then_inc(c_in, 16)
            sp.dma_start(brb[:], a["b_router"].to_broadcast([P, G + NE])).then_inc(c_in, 16)
            for cc in range(CC):
                sp.dma_start(us[:, cc, :, 0:HIST], a["state_conv"][:, cc]).then_inc(hist_in, 16)
            for c in range(CC):
                if c + 1 < CC:
                    sp.wait_ge(wcv_lo, c + 1)
                    sp.dma_start(wcv_raw, a["w_cv"][c + 1]).then_inc(wcv_in, 16)
                w_pieces(sp, c, load_wt)
            sp.wait_ge(zero, 1)
            for half in range(2):
                sp.dma_start(a["yrows"][NE * P:NTILE * P, half * 512:(half + 1) * 512].rearrange("(t p) w -> p t w", p=P),
                             PT[:].rearrange("p a b -> p (a b)").unsqueeze(1).to_broadcast([P, EXTRA, 512])
                             ).then_inc(y_zero, 16)
            sp.wait_ge(u_rdy, 2 * CC)
            sp.wait_ge(hist_in, 16 * CC)
            sp.dma_start(o["conv_prompt"], u[:, :, SEQ:SEQ + HIST]).then_inc(cst_out, 16)
            for c in range(CC):
                sp.dma_start(o["conv_sample"][:, c], us[:, c, :, TB:TB + HIST]).then_inc(cst_out, 16)
            sp.wait_ge(og_ps, NT)
            sp.wait_ge(sconv, 2 * K)
            for k in range(KC):
                if k >= 4 and k % 2 == 0:
                    sp.wait_ge(wl_lo, k - 2)
                if k == 4:
                    sp.dma_start(s0, a["state_gla"]).then_inc(s0_in, 16)
                sp.dma_start(wo_raw[k % 4], a["w_out"][:, k]).then_inc(wo_in[k // 2 % 2], 16)
            sp.wait_ge(xs_rdy, NT)
            sp.dma_start(g1[:], a["g_ffn"].to_broadcast([P, D])).then_inc(g2_in, 16)
            sp.wait_ge(S_rdy, NT - 1)
            sp.dma_start(o["gla_prompt"], St[:]).then_inc(out_st, 16)
            def mix_io(n, j):
                if not late(n, 1):
                    sp.wait_ge(wl_lo, KC)
                if late(n, 2):
                    sp.wait_ge(h_rdy, n - 1)
                sp.dma_start(side[j][:].rearrange("p a b -> p (a b)"), rows(a["x"], n)).then_inc(x2_in[j], 16)

            def xn2_store(n, j):
                sp.wait_ge(xn2_rdy, n + 1)
                sp.dma_start(rows(a["xn2"], n), xn2[j]).then_inc(xn2_out[j], 16)

            mix_io(0, 0)
            mix_io(1, 1)
            sp.wait_ge(SU_out, NB)
            sp.dma_start(o["gla_sample"], s0).then_inc(out_st, 16)
            with sp.Fori(1, (NT - 1) // 2) as i:
                for j in range(2):
                    xn2_store(2 * i + j - 2, j)
                    mix_io(2 * i + j, j)
            xn2_store(NT - 3, 0)
            mix_io(NT - 1, 0)
            xn2_store(NT - 2, 1)

            def weights(t, sl):
                if late(t, 3):
                    sp.wait_ge(gu_ps, t - 2)
                sp.dma_start(wgu[sl], a["w_gu"][bass.ds(t, 1)].rearrange("a p k f -> (a p) k f")).then_inc(gu_in[sl], 16)
                if late(t, 3):
                    sp.wait_ge(y_ps, t - 2)
                sp.dma_start(wdn[sl], a["w_dn"][bass.ds(t, 1)].rearrange("a p k f -> (a p) k f")).then_inc(dn_in[sl], 16)

            def y_store(t, sl):
                sp.wait_ge(y_a, t + 1)
                sp.wait_ge(y_v, t + 1)
                sp.dma_start(rows(a["yrows"], t), yt[sl]).then_inc(y_out[sl], 16)

            def load_p(n, j):
                if late(n, 2):
                    sp.wait_ge(pr_ps, n - 1)
                sp.dma_start(pT[j], a["pT"][bass.ds(n, 1)].rearrange("a p k t -> (a p) k t")).then_inc(pT_in[j], 16)

            sp.wait_ge(og_rdy, NT)
            weights(1, 1)
            xn2_store(NT - 1, 0)
            sp.wait_ge(w_ps, 2 * NT)
            weights(0, 0)
            sp.wait_ge(lg_ps, NT)
            sp.dma_start(gfin, a["g_final"].to_broadcast([P, D])).then_inc(pw_in, 16)
            sp.dma_start(g1[:], a["g_ple"].to_broadcast([P, D])).then_inc(pw_in, 16)
            for k in range(6, KC):
                sp.dma_start(wple[k], a["w_ple"][:, k]).then_inc(wple_in, 16)
            load_p(0, 0)
            load_p(1, 1)
            sp.wait_ge(xg_in[1], 16)
            weights(2, 2)

            def expert_io(t, sl):
                y_store(t, sl)
                weights(t + 3, sl)

            with sp.Fori(0, (NE - 5) // 3) as i:
                for sl in range(3):
                    expert_io(3 * i + sl, sl)
            expert_io(NE - 5, 0)
            expert_io(NE - 4, 1)
            y_store(NE - 3, 2)
            sp.wait_ge(pos_rdy, 1)
            count = sp.value_load(plan[0:1, EXTRA + 2:EXTRA + 3], min_val=0, max_val=EXTRA)

            def extra_weights(t, sl, done):
                e = sp.value_load(plan[0:1, bass.ds(t, 1)], min_val=0, max_val=NE - 1)
                sp.wait_ge(gu_ps, done)
                sp.dma_start(wgu[sl], a["w_gu"][bass.ds(e, 1)].rearrange("a p k f -> (a p) k f")).then_inc(gu_in[sl], 16)
                sp.wait_ge(y_ps, done)
                sp.dma_start(wdn[sl], a["w_dn"][bass.ds(e, 1)].rearrange("a p k f -> (a p) k f")).then_inc(dn_in[sl], 16)

            with sp.If(count > 0):
                extra_weights(0, 2, NE - 2)
            y_store(NE - 2, 0)
            with sp.If(count > 1):
                extra_weights(1, 1, NE)
            y_store(NE - 1, 1)

            def load_ple():
                for k in range(6):
                    sp.dma_start(wple[k], a["w_ple"][:, k]).then_inc(wple_in, 16)

            def load_proj():
                sp.dma_start(wproj, a["w_proj"]).then_inc(pw_in, 16)

            with sp.If(count < 2):
                load_ple()
                with sp.If(count < 1):
                    load_proj()

            def extra_io(t, sl):
                with sp.If(count > t + 2):
                    extra_weights(t + 2, sl, t + NE + 1)
                with sp.If(count == t + 2):
                    load_ple()
                y_store(t + NE, sl)
                sp.wait_ge(y_out[3 - sl], extra_turn(t - 1, 3 - sl))
                hold(sp, passed)
                with sp.If(count == t + 1):
                    load_proj()
                    sp.wait_ge(y_out[sl], extra_turn(t, sl))
                    hold(sp, passed)

            extra(sp, count, extra_io)
            for sl in range(3):
                sp.wait_ge(y_out[sl], 16 * ((NE + 2 - sl) // 3))
            sp.sem_inc(y_all, 1)


            def y_final(n, j):
                sp.wait_ge(y_rdy, n + 1)
                sp.dma_start(rows(o["y"], n), yo[j]).then_inc(fin_out[j], 16)

            with sp.Fori(0, (NT - 3) // 2) as i:
                for j in range(2):
                    y_final(2 * i + j, j)
                    load_p(2 * i + j + 2, j)
            y_final(NT - 3, 0)
            load_p(NT - 1, 0)
            y_final(NT - 2, 1)
            y_final(NT - 1, 0)
            sp.wait_ge(fin_out[0], 16 * 5)
            sp.wait_ge(fin_out[1], 16 * 4)
            sp.wait_ge(out_st, 32)

        @block.gpsimd
        def _(pl):
            pl.memset(eps[:], EPS)
            pl.memset(PT[:], 0.0)
            pl.memset(u[:, :, 0:HIST], 0.0)
            pl.memset(lrT[:], 1.0)
            pl.memset(St[:], 0.0).then_inc(zero, 1)
            def split_cv(c):
                pl.wait_ge(wcv_hi, c + 1)
                pl.tensor_tensor(wcv[c % 2][1], wcv_raw, wcv[c % 2][0], ALU.subtract).then_inc(wcv_lo, 1)

            def split_wt(k, half):
                pl.wait_ge(wt_hi, 2 * k + half + 1)
                hi, lo = [w[:, bass.ds(k, 1), half * TH:(half + 1) * TH].rearrange("p a f -> p (a f)") for w in wtok]
                pl.tensor_tensor(lo, wt_raw[half], hi, ALU.subtract).then_inc(wt_lo, 1)

            split_cv(0)
            for c in range(CC):
                if c + 1 < CC:
                    split_cv(c + 1)
                w_pieces(pl, c, split_wt)
                pl.wait_ge(cv_sb, 6 * (c + 1))
                pl.tensor_tensor(u[:, c, HIST:UW], a_sb[:, 0:SEQ], sg_sb[:, 0:SEQ], ALU.mult).then_inc(u_rdy, 1)
                pl.tensor_tensor(us[:, c, :, HIST:SW], a_sb[:, SEQ:SEQ + NS].rearrange("p (b t) -> p b t", t=TB),
                                 sg_sb[:, SEQ:SEQ + NS].rearrange("p (b t) -> p b t", t=TB), ALU.mult).then_inc(u_rdy, 1)
            pl.wait_ge(u_rdy, 2 * CC)
            pl.memset(oraw[NS:P, NT - 1, :], 0.0).then_inc(zero, 1)

            def state_scaled(n, j):
                pl.wait_ge(E_rdy, n + 1)
                if late(n, 1):
                    pl.wait_ge(S_rdy, n)
                pl.wait_ge(sconv, min(10 * n + 2, 2 * K) if isinstance(n, int) else 10 * n + 2)
                pl.tensor_tensor(Smid[:], St[:], EL[j][:, :, 0:1].to_broadcast([DK, H, DV]), ALU.mult).then_inc(Sm_rdy, 1)
                pl.wait_ge(Sm_rdy, 2 * n + 1)
                pl.tensor_tensor(Slast[:], Smid[:], EL[j][:, :, 1:2].to_broadcast([DK, H, DV]), ALU.mult).then_inc(Sm_rdy, 1)

            accs = cT[:, :, SEQ:SEQ + NS].rearrange("p c (b t) -> p c b t", t=TB)

            def over_samples(v):
                return v.unsqueeze(3).to_broadcast([P, CC, NB, TB])

            def sample_tap(k):
                if late(k, 1):
                    pl.wait_ge(sconv, 2 * k)
                pl.tensor_tensor(sprod, us[:, :, :, bass.ds(k, TB)], over_samples(wc[:, :, bass.ds(k, 1)]),
                                 ALU.mult).then_inc(sconv, 1)
                pl.wait_ge(sconv, 2 * k + 1)
                if late(k, 1):
                    pl.tensor_tensor(accs, accs, sprod, ALU.add).then_inc(sconv, 1)
                else:
                    pl.tensor_tensor(accs, sprod, over_samples(cvec[:, 0, :].unsqueeze(2)), ALU.add).then_inc(sconv, 1)

            def gla(n, j):
                state_scaled(n, j)
                pl.wait_ge(Sm_rdy, 2 * n + 2)
                for q in range(5):
                    sample_tap(5 * n + q + 1)

            pl.wait_ge(zero, 2)
            pl.wait_ge(hist_in, 16 * CC)
            pl.wait_ge(c_in, 16 * (len(SMALL) + 1))
            sample_tap(0)
            gla(0, 0)
            gla(1, 1)
            with pl.Fori(1, 3) as i:
                gla(2 * i, 0)
                gla(2 * i + 1, 1)
            state_scaled(6, 0)
            state_scaled(7, 1)
            pl.wait_ge(og_ps, NT)
            pl.memset(qm, 0.0).then_inc(zero, 1)
            pl.wait_ge(zero, 3)
            pl.wait_ge(qT_rdy, NT)
            for hd in range(H):
                for b in range(NB):
                    pl.tensor_copy(qm[:, hd, b, b * TB:(b + 1) * TB], qkT[:, hd, b * TB:(b + 1) * TB])
            for b in range(NB):
                x = pl.tensor_scalar(km[:, b, :], qk[:, QW:2 * QW], C["seqone"][:, b:b + 1], None, ALU.mult)
            x.then_inc(smp, 1)

            def conv_tile(n, j):
                if late(n, 2):
                    pl.wait_ge(w_ps, 2 * n - 2)
                tile = cT[:, :, bass.ds(n * P, P)]
                pl.tensor_copy(catT[j][0][:, CC:KC, :], tile).then_inc(catT_c, 1)
                pl.wait_ge(catT_c, 2 * n + 1)
                hold(pl, passed)
                pl.tensor_tensor(catT[j][1][:, CC:KC, :], tile, catT[j][0][:, CC:KC, :], ALU.subtract).then_inc(catT_c, 1)

            pl.wait_ge(ln_v, 3)
            for c in range(2, CC):
                pl.tensor_tensor(cT[:, c, :], cT[:, c, :], mean, ALU.subtract).then_inc(ln_psub, 1)
            pl.wait_ge(cT_rdy, CC)
            tiles(pl, conv_tile)

            pl.wait_ge(ids_rdy, 1)
            pl.wait_ge(xn2_out[0], 16 * 5)
            pl.wait_ge(xn2_out[1], 16 * 4)

            def gather(t, sl):
                if late(t, 3):
                    pl.wait_ge(xgT_ps, t - 2)
                pl.tensor_copy(idx[sl][:], ids[:, bass.ds(t, 1)]).then_inc(idx_rdy, 1)
                pl.wait_ge(idx_rdy, t + 1)
                hold(pl, passed)
                pl.indirect_dma_start(xg[sl], None, a["xn2"], bass.IndirectOffsetOnAxis(idx[sl][:], 0)).then_inc(xg_in[sl], 16)

            gather(0, 0)
            gather(1, 1)
            gather(2, 2)
            with pl.Fori(1, (NE - 2) // 3) as i:
                for sl in range(3):
                    gather(3 * i + sl, sl)
            gather(NE - 2, 0)
            gather(NE - 1, 1)
            count = pl.value_load(plan[0:1, EXTRA + 2:EXTRA + 3], min_val=0, max_val=EXTRA)

            def gather_extra(t, sl):
                pl.wait_ge(xgT_ps, t + NE - 1)
                pl.tensor_copy(idx[sl][:], ids[:, bass.ds(t + NE, 1)]).then_inc(idx_rdy, 1)
                pl.wait_ge(idx_rdy, t + NE + 1)
                hold(pl, passed)
                pl.indirect_dma_start(xg[sl], None, a["xn2"], bass.IndirectOffsetOnAxis(idx[sl][:], 0)).then_inc(xg_in[sl], 16)

            extra(pl, count, gather_extra)

            pl.wait_ge(y_all, 1)
            pl.wait_ge(moe_done, 1)

            def gather_y(n, j):
                if late(n, 2):
                    pl.wait_ge(add_rdy, 2 * n - 2)
                for m in range(2):
                    pl.tensor_copy(idy[j][m][:], posY[:, bass.ds(n + m * NT, 1)]).then_inc(idy_rdy, 1)
                    pl.wait_ge(idy_rdy, 2 * n + m + 1)
                    hold(pl, passed)
                    pl.indirect_dma_start(yg[j][m], None, a["yrows"],
                                          bass.IndirectOffsetOnAxis(idy[j][m][:], 0)).then_inc(yg_in[j][m], 16)

            tiles(pl, gather_y)

        @block.scalar
        def _(act):
            def norm_x(n, j):
                act.wait_ge(x_in[j], 8 * (n - j) + 16)
                act.activation(sqj[j], xt[:, bass.ds(n, 1), :].rearrange("p a b -> p (a b)"), ACT.Square,
                               accum_out=ssq[:, j:j + 1]).then_inc(ssq_rdy, 1)
                act.wait_ge(ssq_rdy, n + 1)
                if late(n, 2):
                    act.wait_ge(rst_rdy, n - 1)
                act.activation(std[:, j:j + 1], ssq[:, j:j + 1], ACT.Sqrt, scale=1.0 / D,
                               bias=eps[:, 0:1]).then_inc(std_rdy, 1)

            def evac_xT(n, j):
                act.wait_ge(xT_ps, n + 1)
                act.activation(xnT[0][:, :, bass.ds(n * P, P)],
                               psum[:, 4 + 2 * j:6 + 2 * j, :].rearrange("p a (b c) -> p (a b) c", c=P),
                               ACT.Copy).then_inc(xnT_a, 1)

            def split_cv(c):
                act.wait_ge(wcv_in, 16 * (c + 1))
                if c >= 2:
                    act.wait_ge(cv_ps, 6 * (c - 1))
                act.activation(wcv[c % 2][0], wcv_raw, ACT.Copy).then_inc(wcv_hi, 1)

            def warm(fn, col):
                act.activation(E1[:, col:col + 1], eps[:, 0:1], fn)

            act.wait_ge(zero, 1)
            warm(ACT.Sqrt, 0)
            norm_x(0, 0)
            norm_x(1, 1)
            with act.Fori(1, (NT - 1) // 2) as i:
                for j in range(2):
                    norm_x(2 * i + j, j)
                    evac_xT(2 * i + j - 2, j)
            norm_x(NT - 1, 0)
            evac_xT(NT - 3, 0)
            split_cv(0)
            evac_xT(NT - 2, 1)
            evac_xT(NT - 1, 0)

            def split_wt(k, half):
                act.wait_ge(wt_in[half], 16 * k + 16)
                act.activation(wtok[0][:, bass.ds(k, 1), half * TH:(half + 1) * TH].rearrange("p a f -> p (a f)"),
                               wt_raw[half], ACT.Copy).then_inc(wt_hi, 1)

            act.wait_ge(xs_rdy, NT)
            for c in range(CC):
                if c + 1 < CC:
                    split_cv(c + 1)
                w_pieces(act, c, split_wt)
                if c >= 1:
                    act.wait_ge(u_rdy, 2 * c)
                for part, (dst, fn) in enumerate([(sg_sb, ACT.Sigmoid), (a_sb, ACT.Copy)]):
                    for b in range(NBLK):
                        act.wait_ge(cv_ps, 6 * c + 3 * part + b + 1)
                        act.activation(dst[:, b * BLK:(b + 1) * BLK], psum[:, 3 * part + b, 0:BLK], fn).then_inc(cv_sb, 1)

            def lr_out(n):
                act.wait_ge(lr_ps, n + 1)
                act.activation(lr_sb[:], bk["lr"][:, 0:LR], ACT.Copy).then_inc(lr_rdy, 1)

            def lrT_out(n):
                act.wait_ge(lrT_ps, n + 1)
                act.activation(lrT[0:LR, :], bk["lr"][0:LR, LR:LR + P], ACT.Copy).then_inc(lrT_rdy, 1)

            def log_gate(n):
                act.wait_ge(lap_ps, n + 1)
                act.activation(absx[:], bk["lr"][:, 144:400], ACT.Abs).then_inc(absx_rdy, 1)
                act.wait_ge(absx_rdy, 3 * n + 1)
                act.activation(absx[:], absx[:], ACT.Exp, scale=-1.0).then_inc(absx_rdy, 1)
                act.wait_ge(absx_rdy, 3 * n + 2)
                act.activation(absx[:], absx[:], ACT.Ln, bias=1.0).then_inc(absx_rdy, 1)

            def v_out(n, j):
                act.wait_ge(v_ps, n + 1)
                if late(n, 2):
                    act.wait_ge(U_ps, n - 1)
                act.activation(v_sb[j][:], bk["v"], ACT.Copy).then_inc(v_rdy, 1)

            def decays(n, j):
                act.wait_ge(b_ps, n + 1)
                act.activation(E1[:], bk["lr"][:, 144:400], ACT.Exp)
                act.activation(E2[:], bk["lr"][:, 144:400], ACT.Exp, scale=-1.0)
                if isinstance(n, int) and n == NT - 1:
                    x = act.activation(ELs[:].rearrange("p h b -> p (h b)"), bk["lr"][0:DK, 400:400 + H * NB], ACT.Exp)
                else:
                    if late(n, 2):
                        act.wait_ge(S_rdy, n - 1)
                    x = act.activation(EL[j][:].rearrange("p h b -> p (h b)"), bk["lr"][0:DK, 400:400 + 2 * H], ACT.Exp)
                x.then_inc(E_rdy, 1)

            def gate_tanh(n):
                act.wait_ge(og_ps, n + 1)
                if late(n, 1):
                    act.wait_ge(gog_rdy, n)
                act.activation(th[:], bk["og"], ACT.Tanh, scale=0.5).then_inc(th_rdy, 1)

            def kT_out(n):
                act.wait_ge(qkT_ps, n + 1)
                act.activation(qkT[:, H:2 * H, :], bk["kT"][0:DK, :].rearrange("p (a b) -> p a b", b=P),
                               ACT.Copy).then_inc(kT_rdy, 1)

            def o_out(n, m=P):
                act.wait_ge(o_ps, n + 1)
                act.activation(oraw[0:m, bass.ds(n, 1), :], bk["o"][0:m, :].rearrange("p (a b) -> p a b", a=1),
                               ACT.Copy).then_inc(o_rdy, 1)

            def gla(n, j):
                lr_out(n + 1)
                kT_out(n)
                lrT_out(n + 1)
                log_gate(n + 1)
                v_out(n + 1, 1 - j)
                decays(n + 1, 1 - j)
                o_out(n)
                gate_tanh(n + 1)

            lr_out(0)
            lrT_out(0)
            log_gate(0)
            v_out(0, 0)
            decays(0, 0)
            gate_tanh(0)
            gla(0, 0)
            with act.Fori(0, 3) as i:
                gla(2 * i + 1, 1)
                gla(2 * i + 2, 0)
            gla(NT - 2, 1)

            def split_wo(k):
                act.wait_ge(wo_in[k // 2 % 2], 32 * (k // 4 + 1))
                act.activation(wout[0][:, k, :], wo_raw[k % 4], ACT.Copy).then_inc(wl_hi, 1)

            kT_out(NT - 1)
            split_wo(0)
            split_wo(1)

            def o_square(n, j):
                for hd in range(H):
                    x = act.activation(th[:, hd * DV:(hd + 1) * DV], oraw[:, bass.ds(n, 1), hd * DV:(hd + 1) * DV]
                                       .rearrange("p a b -> p (a b)"), ACT.Square,
                                       accum_out=osq[:, j, hd:hd + 1])
                x.then_inc(osq_rdy, 1)
                act.wait_ge(osq_rdy, n + 1)
                act.activation(ostd[:, j, :], osq[:, j, :], ACT.Sqrt, scale=1.0 / DV,
                               bias=eps[:, 0:1]).then_inc(ostd_rdy, 1)

            def oT_out(n, j):
                act.wait_ge(oT_ps, n + 1)
                act.activation(catT[j][0][:, 0:H, :], psum[:, 4, :].rearrange("p (a b) -> p a b", b=P), ACT.Copy,
                               scale=gghalf[:, 0:1]).then_inc(catT_o, 1)

            for c in range(CC):
                if c == 0:
                    act.wait_ge(conv, K * CC)
                    act.wait_ge(sconv, 2 * K)
                    act.wait_ge(cst_out, 16 * (CC + 1))
                act.activation(csq[:, c, :], cT[:, c, :], ACT.Square).then_inc(csq_rdy, 1)
            for k in range(2, KC):
                split_wo(k)
            act.wait_ge(gog_rdy, NT)
            o_square(0, 0)
            o_square(1, 1)
            act.wait_ge(ln_v, 3)
            act.activation(rstdb, rstdb, ACT.Sqrt, bias=eps[:, 0:1]).then_inc(ln_std, 1)
            oT_out(0, 0)
            o_out(NT - 1, NS)
            oT_out(1, 1)
            warm(ACT.Silu, 1)
            for c in range(CC):
                act.wait_ge(ln_x, c + 1)
                act.activation(cT[:, c, :], cT[:, c, :], ACT.Silu, scale=cvec[:, 1, c:c + 1],
                               bias=cvec[:, 2, c:c + 1]).then_inc(cT_rdy, 1)

            def xn2T_out(n, j):
                act.wait_ge(xn2T_ps, n + 1)
                act.activation(xn2T[j][:, 0:4, :], psum[:, 5, :].rearrange("p (a b) -> p a b", b=P),
                               ACT.Copy).then_inc(xn2T_a, 1)

            def h_square(n, j):
                act.wait_ge(h_rdy, n + 1)
                if late(n, 2):
                    act.wait_ge(xn2_out[j], 8 * (n - j))
                act.activation(xn2[j], h[:, bass.ds(n, 1), :].rearrange("p a b -> p (a b)"), ACT.Square,
                               accum_out=ssq[:, j:j + 1]).then_inc(ssq_rdy, 1)
                act.wait_ge(ssq_rdy, NT + n + 1)
                act.activation(std[:, j:j + 1], ssq[:, j:j + 1], ACT.Sqrt, scale=1.0 / D,
                               bias=eps[:, 0:1]).then_inc(std_rdy, 1)

            def mix(n, j):
                last = isinstance(n, int) and n == NT - 1
                first = isinstance(n, int) and n == 0
                if not last and not first:
                    o_square(n + 1, 1 - j)
                if late(n, 1):
                    xn2T_out(n - 1, 1 - j)
                if not last and not first:
                    oT_out(n + 1, 1 - j)
                h_square(n, j)

            tiles(act, mix)
            xn2T_out(NT - 1, 0)

            act.wait_ge(gd_rdy, 1)
            act.activation(gsc, gd, ACT.Exp).then_inc(ge_rdy, 1)
            act.wait_ge(dv_rdy, 1)
            act.activation(one["ev"], one["dv"], ACT.Exp).then_inc(ev_rdy, 1)
            warm(ACT.Silu, 2)

            def halfT(dst, bank, sem_):
                act.activation(dst[:, 0:4, :], psum[:, bank, :].rearrange("p (a b) -> p a b", b=P), ACT.Copy).then_inc(sem_, 1)

            def xgT_out(t, sl):
                act.wait_ge(xgT_ps, t + 1)
                halfT(xgT[sl], 0, xgT_a)

            def silu(t, sl):
                act.wait_ge(gu_ps, t + 1)
                if late(t, 3):
                    act.wait_ge(hg_rdy, t - 2)
                act.activation(sil[sl], psum[:, 2 + sl, 0:FF], ACT.Silu).then_inc(sil_rdy, 1)

            def y_half(t, sl, stored=None):
                act.wait_ge(y_ps, t + 1)
                if stored is not None or late(t, 3):
                    act.wait_ge(y_out[sl], turn_of(t, sl) * 16 if stored is None else stored)
                act.activation(yt[sl][:, 0:512], psum[:, 6, :], ACT.Copy).then_inc(y_a, 1)

            def expert(t, sl):
                silu(t, sl)
                if isinstance(t, int) and t == NE - 1:
                    with act.If(count > 0):
                        xgT_out(NE, 2)
                else:
                    xgT_out(t + 1, (sl + 1) % 3)
                if late(t, 1):
                    y_half(t - 1, (sl - 1) % 3)

            act.wait_ge(pos_rdy, 1)
            count = act.value_load(plan[0:1, EXTRA + 2:EXTRA + 3], min_val=0, max_val=EXTRA)
            xgT_out(0, 0)
            experts(act, expert)
            with act.If(count == 0):
                y_half(NE - 1, (NE - 1) % 3)

            def expert_extra(t, sl):
                act.wait_ge(gu_ps, t + NE + 1)
                act.wait_ge(hg_rdy, t + NE - 1)
                act.activation(sil[sl], psum[:, 2 + sl, 0:FF], ACT.Silu).then_inc(sil_rdy, 1)
                with act.If(count > t + 1):
                    xgT_out(t + NE + 1, 3 - sl)
                y_half(t + NE - 1, 3 - sl, extra_turn(t - 1, 3 - sl) - 16)
                with act.If(count == t + 1):
                    y_half(t + NE, sl, extra_turn(t, sl) - 16)

            extra(act, count, expert_extra)

            def h_square3(n, j):
                act.wait_ge(add_rdy, 2 * n + 2)
                act.activation(xn3[j], h[:, bass.ds(n, 1), :].rearrange("p a b -> p (a b)"), ACT.Square,
                               accum_out=ssq[:, j:j + 1]).then_inc(ssq_rdy, 1)
                act.wait_ge(ssq_rdy, 2 * NT + n + 1)
                act.activation(std[:, j:j + 1], ssq[:, j:j + 1], ACT.Sqrt, scale=1.0 / D,
                               bias=eps[:, 0:1]).then_inc(std3_rdy, 1)

            def x3T_out(n, j):
                act.wait_ge(x3T_ps, n + 1)
                act.activation(x3T[j][0], psum[:, 0:2, :].rearrange("p a (b c) -> p (a b) c", c=P), ACT.Copy).then_inc(x3T_a, 1)

            def gate_sig(n, j):
                act.wait_ge(gt_ps, 2 * n + 2)
                if late(n, 2):
                    act.wait_ge(y_rdy, n - 1)
                act.activation(mixd[j].rearrange("p (a b) -> p a b", b=512), psum[:, 2 + 4 * j:4 + 4 * j, :],
                               ACT.Sigmoid).then_inc(sg_rdy, 1)

            def out_square(n, j):
                act.wait_ge(mix_rdy, 2 * n + 2)
                if late(n, 2):
                    act.wait_ge(fin_out[j], 8 * (n - j))
                act.activation(yo[j], mixd[j], ACT.Square, accum_out=ssq[:, j:j + 1]).then_inc(ssq4_rdy, 1)
                act.wait_ge(ssq4_rdy, n + 1)
                act.activation(std[:, j:j + 1], ssq[:, j:j + 1], ACT.Sqrt, scale=1.0 / D,
                               bias=eps[:, 0:1]).then_inc(std4_rdy, 1)

            def embed(n, j):
                if not (isinstance(n, int) and n == NT - 1):
                    x3T_out(n + 1, 1 - j)
                if not (isinstance(n, int) and n >= NT - 2):
                    h_square3(n + 2, j)
                gate_sig(n, j)
                out_square(n, j)

            warm(ACT.Sqrt, 3)
            act.wait_ge(moe_done, 1)
            act.wait_ge(wple_in, 16 * KC)
            for k in range(KC):
                if k == 3:
                    act.wait_ge(y_all, 1)
                if k >= 6:
                    act.wait_ge(wl_lo, KC + k - 5)
                act.activation(wgate[k][0][:, 0, :], wple[k], ACT.Copy).then_inc(wl_hi, 1)
            h_square3(0, 0)
            x3T_out(0, 0)
            h_square3(1, 1)
            embeds(act, embed)

        @block.vector
        def _(dve):
            dve.wait_ge(g1_in, 32)

            def norm_x(n, j):
                dve.wait_ge(std_rdy, n + 1)
                dve.reciprocal(rst[:, j:j + 1], std[:, j:j + 1]).then_inc(rst_rdy, 1)
                dve.wait_ge(rst_rdy, n + 1)
                if late(n, 2):
                    dve.wait_ge(xT_ps, n - 1)
                dve.scalar_tensor_tensor(xs[j], xt[:, bass.ds(n, 1), :].rearrange("p a b -> p (a b)"), rst[:, j:j + 1],
                                         g1[:], ALU.mult, ALU.mult).then_inc(xs_rdy, 1)

            def evac_xT(n, j):
                dve.wait_ge(xnT_a, n + 1)
                tile = bass.ds(n * P, P)
                dve.tensor_tensor(xnT[1][:, :, tile], psum[:, 4 + 2 * j:6 + 2 * j, :].rearrange("p a (b c) -> p (a b) c", c=P),
                                  xnT[0][:, :, tile], ALU.subtract).then_inc(xnT_v, 1)

            norm_x(0, 0)
            norm_x(1, 1)
            with dve.Fori(1, (NT - 1) // 2) as i:
                for j in range(2):
                    norm_x(2 * i + j, j)
                    evac_xT(2 * i + j - 2, j)
            norm_x(NT - 1, 0)
            evac_xT(NT - 3, 0)
            evac_xT(NT - 2, 1)
            evac_xT(NT - 1, 0)
            dve.wait_ge(c_in, 16 * (len(SMALL) + 1))
            dve.tensor_copy(upper16[:], C["upper"])
            dve.tensor_copy(ones16[:], C["ones"])
            dve.tensor_scalar(gghalf[:], ggo[:], 0.5, None, ALU.mult)

            dve.wait_ge(zero, 1)
            def taps(c, first, count, done):
                w = wc[:, bass.ds(c, 1), :].rearrange("p a k -> p (a k)")
                acc = cT[:, bass.ds(c, 1), 0:SEQ].rearrange("p a t -> p (a t)")
                for k in range(first, first + count):
                    src = u[:, bass.ds(c, 1), k:k + SEQ].rearrange("p a t -> p (a t)")
                    if k == 0:
                        dve.wait_ge(u_rdy, 2 * (c + 1))
                        b = cvec[:, 0, bass.ds(c, 1)]
                        dve.tensor_scalar(acc, src, w[:, 0:1], b, ALU.mult, ALU.add).then_inc(conv, 1)
                    else:
                        dve.wait_ge(conv, done + k - first)
                        dve.scalar_tensor_tensor(acc, src, w[:, k:k + 1], acc, ALU.mult, ALU.add).then_inc(conv, 1)

            dve.memset(cT[:, :, SEQ + NS:TOK], 0.0)
            REST = 9
            BESIDE = (K + REST) // 4
            with dve.Fori(0, CC // 2) as c:
                taps(c, 0, K - REST, (K - REST) * c)

            def taps_beside(i, first, count):
                done = 2 * (K - REST) + (K + REST) * i + first
                old = max(min(REST - first, count), 0)
                if old:
                    taps(i, K - REST + first, old, done)
                if count > old:
                    taps(i + CC // 2, first + old - REST, count - old, done + old)

            def log_gate(n):
                dve.wait_ge(absx_rdy, 3 * n + 3)
                dve.scalar_tensor_tensor(la[:], bk["lr"][:, 144:400], 0.0, absx[:], ALU.min, ALU.subtract).then_inc(la_rdy, 1)

            def decay_qk(n):
                dve.wait_ge(E_rdy, n + 1)
                dve.wait_ge(qk_ps, n + 1)
                dve.scalar_tensor_tensor(qk[:, 0:QW], bk["qk"][:, 0:QW], DK ** -0.5, E1[:], ALU.mult, ALU.mult)
                dve.tensor_tensor(qk[:, QW:2 * QW], bk["qk"][:, QW:2 * QW], E2[:], ALU.mult).then_inc(qk_rdy, 1)

            def gate(n):
                dve.wait_ge(th_rdy, n + 1)
                dve.scalar_tensor_tensor(gog[:, bass.ds(n, 1), :].rearrange("p a b -> p (a b)"), th[:], 1.0, bk["og"],
                                         ALU.add, ALU.mult).then_inc(gog_rdy, 1)

            def qT_out(n):
                dve.wait_ge(qkT_ps, n + 1)
                dve.tensor_copy(qkT[:, 0:H, :], bk["qT"][0:DK, :].rearrange("p (a b) -> p a b", b=P)).then_inc(qT_rdy, 1)

            def mask_scores(n, m):
                dve.wait_ge(sc_ps, n + 1)
                dve.tensor_tensor(PT[:], bk["sc"].rearrange("p (a b) -> p a b", b=P),
                                  m.unsqueeze(1).to_broadcast([P, H, P]), ALU.mult).then_inc(PT_rdy, 1)

            def state(n, j):
                dve.wait_ge(U_ps, n + 1)
                dve.wait_ge(Sm_rdy, 2 * n + 2)
                for hd in range(H):
                    x = dve.scalar_tensor_tensor(St[:, hd, :], bk["qT"][0:DK, hd * DV:(hd + 1) * DV], EL[j][:, hd, 1:2],
                                                 Slast[:, hd, :], ALU.mult, ALU.add)
                x.then_inc(S_rdy, 1)

            dve.wait_ge(y_zero, 32)

            def gla(n, j, i, first):
                qT_out(n)
                taps_beside(i, first, 3)
                mask_scores(n, C["cmask"])
                log_gate(n + 1)
                taps_beside(i, first + 3, 3)
                state(n, j)
                decay_qk(n + 1)
                taps_beside(i, first + 6, BESIDE - 6)
                gate(n + 1)

            log_gate(0)
            decay_qk(0)
            dve.wait_ge(u_rdy, 2 * CC)
            gate(0)
            with dve.Fori(0, 2) as i:
                for r in range(4):
                    gla(4 * i + r, r % 2, i, BESIDE * r)
            qT_out(NT - 1)
            mask_scores(NT - 1, C["cmasks"])
            for k in range(KC):
                dve.wait_ge(wl_hi, k + 1)
                dve.tensor_tensor(wout[1][:, k, :], wo_raw[k % 4], wout[0][:, k, :], ALU.subtract).then_inc(wl_lo, 1)

            def o_norm(n, j):
                dve.wait_ge(ostd_rdy, n + 1)
                dve.reciprocal(orst[:, j, :], ostd[:, j, :]).then_inc(orst_rdy, 1)
                dve.wait_ge(orst_rdy, n + 1)
                if late(n, 2):
                    dve.wait_ge(oT_ps, n - 1)
                for hd in range(H):
                    cols = slice(hd * DV, (hd + 1) * DV)
                    x = dve.scalar_tensor_tensor(og[j][:, cols], oraw[:, bass.ds(n, 1), cols].rearrange("p a b -> p (a b)"),
                                                 orst[:, j, hd:hd + 1],
                                                 gog[:, bass.ds(n, 1), cols].rearrange("p a b -> p (a b)"), ALU.mult, ALU.mult)
                x.then_inc(og_rdy, 1)

            o_norm(0, 0)
            o_norm(1, 1)
            dve.wait_ge(st_ps, 1)
            dve.tensor_scalar(mean.rearrange("p (a b) -> p a b", b=BLK), psum[:, 0:3, 0:BLK], 1.0 / CW, None,
                              ALU.mult).then_inc(ln_v, 1)
            dve.wait_ge(ln_v, 1)
            dve.tensor_tensor(csq[:, 0, :], mean, mean, ALU.mult).then_inc(ln_v, 1)
            dve.wait_ge(ln_v, 2)
            dve.scalar_tensor_tensor(rstdb.rearrange("p (a b) -> p a b", b=BLK), psum[:, 3:6, 0:BLK], 1.0 / CW,
                                     csq[:, 0, :].rearrange("p (a b) -> p a b", b=BLK), ALU.mult, ALU.subtract).then_inc(ln_v, 1)
            def oT_low(n, j):
                dve.wait_ge(catT_o, n + 1)
                dve.scalar_tensor_tensor(catT[j][1][:, 0:H, :], psum[:, 4, :].rearrange("p (a b) -> p a b", b=P),
                                         gghalf[:, 0:1], catT[j][0][:, 0:H, :], ALU.mult, ALU.subtract).then_inc(catT_l, 1)

            for c in range(2):
                dve.tensor_tensor(cT[:, c, :], cT[:, c, :], mean, ALU.subtract).then_inc(ln_sub, 1)
            oT_low(0, 0)
            dve.wait_ge(ln_std, 1)
            dve.reciprocal(rstdb, rstdb).then_inc(ln_v, 1)
            dve.wait_ge(ln_v, 4)
            for c in range(CC):
                if c < 2:
                    dve.wait_ge(ln_sub, c + 1)
                else:
                    dve.wait_ge(ln_psub, c - 1)
                dve.tensor_tensor(cT[:, c, :], cT[:, c, :], rstdb, ALU.mult).then_inc(ln_x, 1)
                if c == 0:
                    oT_low(1, 1)

            dve.wait_ge(s0_in, 16)
            for b in range(NB):
                dve.wait_ge(SU_ps, b + 1)
                dve.tensor_tensor(s0[:, b], psum[0:DK, 5 + b % 3, :].rearrange("p (h d) -> p h d", d=DV), s0[:, b],
                                  ALU.add).then_inc(SU_add, 1)
            for b in range(NB):
                dve.wait_ge(SU_add, b + 1)
                dve.tensor_tensor(s0[:, b], s0[:, b], ELs[:, :, b:b + 1].to_broadcast([DK, H, DV]), ALU.mult).then_inc(SU_out, 1)

            def norm_h(n, j):
                dve.wait_ge(std_rdy, NT + n + 1)
                dve.reciprocal(rst[:, j:j + 1], std[:, j:j + 1]).then_inc(rst_rdy, 1)
                dve.wait_ge(rst_rdy, NT + n + 1)
                dve.scalar_tensor_tensor(xn2[j], h[:, bass.ds(n, 1), :].rearrange("p a b -> p (a b)"), rst[:, j:j + 1],
                                         g1[:], ALU.mult, ALU.mult).then_inc(xn2_rdy, 1)

            def xn2T_out(n, j):
                dve.wait_ge(xn2T_ps, n + 1)
                dve.tensor_copy(xn2T[j][:, 4:8, :], psum[:, 6, :].rearrange("p (a b) -> p a b", b=P)).then_inc(xn2T_v, 1)

            def residual(n, j):
                dve.wait_ge(x2_in[j], 8 * (n - j) + 16)
                dve.wait_ge(w_ps, 2 * n + 2)
                dve.tensor_tensor(h[:, bass.ds(n, 1), :].rearrange("p a b -> p (a b)"),
                                  psum[:, 2 * j:2 * j + 2, :].rearrange("p a b -> p (a b)"),
                                  side[j][:].rearrange("p a b -> p (a b)"), ALU.add).then_inc(h_rdy, 1)

            def logit(n):
                dve.wait_ge(lg_ps, n + 1)
                dve.tensor_tensor(logits[:, bass.ds(n, 1), :].rearrange("p a b -> p (a b)"), psum[:, 7, 0:G + NE], brb[:],
                                  ALU.add).then_inc(lg_rdy, 1)

            dve.wait_ge(g2_in, 16)
            def mix(n, j):
                if late(n, 1):
                    norm_h(n - 1, 1 - j)
                if not (isinstance(n, int) and n in (0, NT - 1)):
                    o_norm(n + 1, 1 - j)
                if late(n, 1):
                    xn2T_out(n - 1, 1 - j)
                if not (isinstance(n, int) and n in (0, NT - 1)):
                    oT_low(n + 1, 1 - j)
                if isinstance(n, int) and n == 1:
                    dve.wait_ge(out_st, 32)
                residual(n, j)
                if late(n, 1):
                    logit(n - 1)

            tiles(dve, mix)
            norm_h(NT - 1, 0)
            xn2T_out(NT - 1, 0)
            logit(NT - 1)

            steps = [0]

            def step(x):
                steps[0] += 1
                x.then_inc(rt, 1)
                dve.wait_ge(rt, steps[0])

            def over(v, n):
                return v.unsqueeze(len(v.shape)).to_broadcast([*v.shape, n])

            def onehot_sum(name, v):
                for m in range(2):
                    x = dve.tensor_tensor(prod[:, m * NT:(m + 1) * NT, :], M12[:, m], v, ALU.mult)
                step(x)
                step(dve.tensor_reduce(two[name], prod, AX, ALU.add))

            def first_max(src, m, ranks, sc, pick, w):
                step(dve.tensor_reduce(m, src, AX, ALU.max))
                step(dve.tensor_tensor(sc, src, over(m, w), ALU.is_equal))
                step(dve.tensor_tensor(sc, sc, C[ranks].unsqueeze(1).to_broadcast([P, NT, w]), ALU.mult))
                step(dve.tensor_reduce(pick, sc, AX, ALU.max))

            gl, el = logits[:, :, 0:G], logits[:, :, G:G + NE].rearrange("p n (g e) -> p n g e", e=E)
            dve.wait_ge(lg_rdy, NT)
            dve.wait_ge(xn2_out[0], 16 * 5)
            dve.wait_ge(xn2_out[1], 16 * 4)
            dve.wait_ge(lg_ps, NT)
            first_max(gl, one["gmax"], "desc4", gsc, one["gm"], G)
            step(dve.tensor_tensor(ohg, gsc, over(one["gm"], G), ALU.is_equal))
            dve.tensor_tensor(gd, gl, over(one["gmax"], G), ALU.subtract).then_inc(gd_rdy, 1)
            gsel = prod[:, 0:NT, :].rearrange("p n (g e) -> p n g e", e=E)
            step(dve.tensor_tensor(gsel, el, over(ohg, E), ALU.mult))
            step(dve.tensor_reduce(sel, gsel.rearrange("p n g e -> p n e g"), AX, ALU.add))
            first_max(sel, one["v1"], "desc8", esc, one["m1"], E)
            step(dve.tensor_tensor(oh[0], esc, over(one["m1"], E), ALU.is_equal))
            step(dve.scalar_tensor_tensor(sel, oh[0], -BIG, sel, ALU.mult, ALU.add))
            first_max(sel, one["v2"], "desc8", esc, one["m2"], E)
            step(dve.tensor_tensor(oh[1], esc, over(one["m2"], E), ALU.is_equal))
            dve.tensor_tensor(one["dv"], one["v2"], one["v1"], ALU.subtract).then_inc(dv_rdy, 1)
            for m in range(2):
                x = dve.tensor_tensor(M12[:, m].rearrange("p n (g e) -> p n g e", e=E), over(ohg, E),
                                      oh[m].unsqueeze(2).to_broadcast([P, NT, G, E]), ALU.mult)
            step(x)
            step(dve.memset(M12[NS:P, :, NT - 1, :], 0.0))
            dve.tensor_tensor(Msum.rearrange("p (e n) -> p n e", n=NT), M12[:, 0], M12[:, 1], ALU.add).then_inc(M_rdy, 1)
            onehot_sum("exp", C["eidx"].unsqueeze(1).to_broadcast([P, NT, NE]))
            step(dve.memset(ovb, 0.0))
            dve.wait_ge(rk_ps, 1)
            step(dve.tensor_tensor_scan(upto, C["inner"], psum[:, 1, 0:NT * NE], 0.0, ALU.mult, ALU.add))
            total = upto.rearrange("p (e n) -> p e n", n=NT)[:, :, NT - 1]
            dve.tensor_tensor(rank, upto, psum[:, 1, 0:NT * NE], ALU.subtract)
            step(dve.tensor_tensor(cmpe, over(total, E), C["steps"].unsqueeze(1).to_broadcast([P, NE, E]), ALU.is_gt))
            step(dve.tensor_tensor(rank, rank, psum[:, 0, 0:NT * NE], ALU.add))
            step(dve.tensor_reduce(nx, cmpe, AX, ALU.add))
            step(dve.tensor_tensor_scan(inc, nx, ovb, 0.0, ALU.add, ALU.add))
            step(dve.tensor_tensor(ovb, inc, nx, ALU.subtract))
            onehot_sum("rank", rank.rearrange("p (e n) -> p n e", n=NT))
            onehot_sum("ovb", ovb.unsqueeze(1).to_broadcast([P, NT, NE]))
            step(dve.tensor_tensor(cmpr, over(two["rank"], E), C["steps"].unsqueeze(1).to_broadcast([P, 2 * NT, E]), ALU.is_ge))
            step(dve.tensor_reduce(two["q"], cmpr, AX, ALU.add))
            step(dve.tensor_scalar(two["isq"], two["q"], 1.0, None, ALU.is_ge))
            step(dve.tensor_tensor(two["t"], two["ovb"], two["q"], ALU.add))
            step(dve.scalar_tensor_tensor(two["t"], two["t"], float(NE - 1), two["exp"], ALU.add, ALU.subtract))
            step(dve.tensor_tensor(two["t"], two["t"], two["isq"], ALU.mult))
            step(dve.tensor_tensor(two["t"], two["t"], two["exp"], ALU.add))
            step(dve.scalar_tensor_tensor(two["r"], two["q"], -float(P), two["rank"], ALU.mult, ALU.add))
            step(dve.scalar_tensor_tensor(two["fy"], two["t"], float(P), two["r"], ALU.mult, ALU.add))
            step(dve.tensor_tensor(oht, over(two["t"], NTILE), C["count"][:, 0:NTILE].unsqueeze(1)
                                   .to_broadcast([P, 2 * NT, NTILE]), ALU.is_equal))
            for m in range(2):
                t = slice(m * NT, (m + 1) * NT)
                dve.tensor_tensor(oht[:, t], oht[:, t], over(C["token"], NTILE), ALU.mult)
                dve.tensor_tensor(ohr[:, t], over(two["r"][:, t], P), C["count"].unsqueeze(1).to_broadcast([P, NT, P]),
                                  ALU.is_equal).then_inc(oh_rdy, 1)
            dve.wait_ge(ids_ps, 1)
            dve.tensor_copy(ids[:], psum[:, 2, 0:NTILE]).then_inc(ids_rdy, 1)
            step(dve.tensor_tensor(cmpt, inc.unsqueeze(1).to_broadcast([P, EXTRA, NE]), over(C["tidx"], NE), ALU.is_le))
            step(dve.tensor_reduce(et, cmpt, AX, ALU.add))
            step(dve.tensor_scalar(plan[:, 0:EXTRA], et, float(NE - 1), None, ALU.min))
            step(dve.tensor_copy(plan[:, EXTRA + 2:EXTRA + 3], inc[:, NE - 1:NE]))
            dve.tensor_copy(posY[:], two["fy"]).then_inc(pos_rdy, 1)
            dve.wait_ge(ge_rdy, 1)
            step(dve.tensor_reduce(one["gsum"], gsc, AX, ALU.add))
            step(dve.reciprocal(one["gw"], one["gsum"]))
            dve.wait_ge(ev_rdy, 1)
            step(dve.tensor_scalar(one["gm"], one["ev"], 1.0, None, ALU.add))
            step(dve.reciprocal(one["gm"], one["gm"]))
            step(dve.tensor_tensor(w12[:, 0, :], one["gm"], one["gw"], ALU.mult))
            step(dve.tensor_tensor(w12[:, 1, :], w12[:, 0, :], one["ev"], ALU.mult))

            def halfT(dst, bank, sem_):
                dve.tensor_copy(dst[:, 4:8, :], psum[:, bank, :].rearrange("p (a b) -> p a b", b=P)).then_inc(sem_, 1)

            def xgT_out(t, sl):
                dve.wait_ge(xgT_ps, t + 1)
                halfT(xgT[sl], 1, xgT_v)

            def glu(t, sl):
                dve.wait_ge(sil_rdy, t + 1)
                dve.tensor_tensor(hg, sil[sl], psum[:, 2 + sl, FF:2 * FF], ALU.mult).then_inc(hg_rdy, 1)

            def hT_out(t):
                dve.wait_ge(hT_ps, t + 1)
                dve.tensor_copy(hT, psum[:, 5, 0:FF].rearrange("p (a b) -> p a b", b=P)).then_inc(hT_rdy, 1)

            def y_half(t, sl, stored=None):
                dve.wait_ge(y_ps, t + 1)
                if stored is not None or late(t, 3):
                    dve.wait_ge(y_out[sl], turn_of(t, sl) * 16 if stored is None else stored)
                dve.tensor_copy(yt[sl][:, 512:D], psum[:, 7, :]).then_inc(y_v, 1)

            def expert(t, sl):
                glu(t, sl)
                if isinstance(t, int) and t == NE - 1:
                    with dve.If(count > 0):
                        xgT_out(NE, 2)
                else:
                    xgT_out(t + 1, (sl + 1) % 3)
                if late(t, 1):
                    y_half(t - 1, (sl - 1) % 3)
                hT_out(t)

            count = dve.value_load(plan[0:1, EXTRA + 2:EXTRA + 3], min_val=0, max_val=EXTRA)
            xgT_out(0, 0)
            experts(dve, expert)
            with dve.If(count == 0):
                y_half(NE - 1, (NE - 1) % 3)

            def expert_extra(t, sl):
                glu(t + NE, sl)
                with dve.If(count > t + 1):
                    xgT_out(t + NE + 1, 3 - sl)
                y_half(t + NE - 1, 3 - sl, extra_turn(t - 1, 3 - sl) - 16)
                hT_out(t + NE)
                with dve.If(count == t + 1):
                    y_half(t + NE, sl, extra_turn(t, sl) - 16)

            extra(dve, count, expert_extra)

            def flat(n):
                return h[:, bass.ds(n, 1), :].rearrange("p a b -> p (a b)")

            def combine(n, j):
                for m in range(2):
                    dve.wait_ge(yg_in[j][m], 8 * (n - j) + 16)
                    if m:
                        dve.wait_ge(add_rdy, 2 * n + 1)
                    dve.scalar_tensor_tensor(flat(n), yg[j][m], w12[:, m, bass.ds(n, 1)], flat(n), ALU.mult,
                                             ALU.add).then_inc(add_rdy, 1)
                dve.wait_ge(std3_rdy, n + 1)
                dve.reciprocal(rst[:, j:j + 1], std[:, j:j + 1]).then_inc(rst3_rdy, 1)
                dve.wait_ge(rst3_rdy, n + 1)
                dve.scalar_tensor_tensor(xn3[j], flat(n), rst[:, j:j + 1], g1[:], ALU.mult, ALU.mult).then_inc(xn3_rdy, 1)

            def x3T_out(n, j):
                dve.wait_ge(x3T_a, n + 1)
                dve.tensor_tensor(x3T[j][1], psum[:, 0:2, :].rearrange("p a (b c) -> p (a b) c", c=P), x3T[j][0],
                                  ALU.subtract).then_inc(x3T_v, 1)

            def finish(n, j):
                dve.wait_ge(sg_rdy, n + 1)
                dve.wait_ge(pr_ps, n + 1)
                dve.tensor_tensor(mixd[j], mixd[j], psum[:, 4:6, :].rearrange("p a b -> p (a b)"), ALU.mult).then_inc(mix_rdy, 1)
                dve.wait_ge(mix_rdy, 2 * n + 1)
                dve.tensor_tensor(mixd[j], mixd[j], flat(n), ALU.add).then_inc(mix_rdy, 1)
                dve.wait_ge(std4_rdy, n + 1)
                dve.reciprocal(rst[:, j:j + 1], std[:, j:j + 1]).then_inc(rst4_rdy, 1)
                dve.wait_ge(rst4_rdy, n + 1)
                dve.scalar_tensor_tensor(yo[j], mixd[j], rst[:, j:j + 1], gfin, ALU.mult, ALU.mult).then_inc(y_rdy, 1)

            def embed(n, j):
                if not (isinstance(n, int) and n == NT - 1):
                    x3T_out(n + 1, 1 - j)
                if not (isinstance(n, int) and n >= NT - 2):
                    combine(n + 2, j)
                finish(n, j)

            dve.wait_ge(moe_done, 1)

            def split_gate(chunks):
                for k in chunks:
                    dve.wait_ge(wl_hi, KC + k + 1)
                    dve.tensor_tensor(wgate[k][1][:, 0, :], wple[k], wgate[k][0][:, 0, :], ALU.subtract).then_inc(wl_lo, 1)

            split_gate(range(KC - 2))
            dve.wait_ge(pw_in, 32)
            combine(0, 0)
            split_gate(range(KC - 2, KC))
            x3T_out(0, 0)
            combine(1, 1)
            embeds(dve, embed)

        @block.tensor
        def _(pe):
            ident = C["ident"]
            PASSES = [(0, 0), (0, 1), (1, 0)]

            pe.wait_ge(g1_in, 32)

            def transpose_x(n, j):
                pe.wait_ge(xs_rdy, n + 1)
                if late(n, 2):
                    pe.wait_ge(xnT_v, n - 1)
                for k in range(KC):
                    x = pe.transpose(psum[:, 4 + 2 * j + k // 4, (k % 4) * P:(k % 4 + 1) * P], xs[j][:, k * P:(k + 1) * P], ident)
                x.then_inc(xT_ps, 1)

            tiles(pe, transpose_x)
            pe.wait_ge(xnT_v, NT)

            for c in range(CC):
                pe.wait_ge(wcv_lo, c + 1)
                for part, col in enumerate([P, 0]):
                    for b in range(NBLK):
                        if c >= 1:
                            pe.wait_ge(cv_sb, 6 * (c - 1) + 3 * part + b + 1)
                        for k in range(KC):
                            for w, m in PASSES:
                                x = pe.matmul(psum[:, 3 * part + b, 0:BLK], wcv[c % 2][w][:, k, col:col + P],
                                              xnT[m][:, k, b * BLK:(b + 1) * BLK], start=k + w + m == 0,
                                              stop=k == KC - 1 and w == 1)
                        x.then_inc(cv_ps, 1)

            def z(n, out, col, width, done):
                for k in range(KC):
                    for w, m in PASSES:
                        x = pe.matmul(out, xnT[w][:, k, bass.ds(n * P, P)], wtok[m][:, k, col:col + width],
                                      start=k + w + m == 0, stop=k == KC - 1 and w == 1)
                x.then_inc(done, 1)

            def z_lr(n):
                z(n, bk["lr"][:, 0:LR], 2 * QW + 2 * VW, LR, lr_ps)

            def z_qk(n):
                z(n, bk["qk"], 0, 2 * QW, qk_ps)

            def z_v(n):
                if late(n, 1):
                    pe.wait_ge(v_rdy, n)
                z(n, bk["v"], 2 * QW, VW, v_ps)

            def z_og(n):
                if late(n, 1):
                    pe.wait_ge(gog_rdy, n)
                z(n, bk["og"], 2 * QW + VW, VW, og_ps)

            def lr_T(n):
                pe.wait_ge(lr_rdy, n + 1)
                pe.transpose(bk["lr"][0:LR, LR:LR + P], lr_sb[:], ident).then_inc(lrT_ps, 1)

            def log_gate(n):
                pe.wait_ge(lrT_rdy, n + 1)
                pe.matmul(bk["lr"][:, 144:400], lrT[:], wf[:], start=True, stop=True).then_inc(lap_ps, 1)

            def cumulate(n):
                samples = isinstance(n, int) and n == NT - 1
                pe.wait_ge(la_rdy, n + 1)
                pe.matmul(bk["lr"][:, 144:400], C["tris" if samples else "tric"], la[:], start=True, stop=True)
                m = C["seqsum" if samples else "halves"]
                w = NB if samples else 2
                for hd in range(H):
                    x = pe.matmul(bk["lr"][0:DK, 400 + w * hd:400 + w * (hd + 1)], la[:, hd * DK:(hd + 1) * DK], m,
                                  start=True, stop=True)
                x.then_inc(b_ps, 1)

            def turn(n):
                pe.wait_ge(qk_rdy, n + 1)
                if late(n, 1):
                    pe.wait_ge(S_rdy, n)
                pe.matmul(bk["qT"][0:DK, 0:P], qk[:, 0:DK], ident, start=True, stop=True)
                for hd in range(1, H):
                    pe.transpose(bk["qT"][0:DK, hd * P:(hd + 1) * P], qk[:, hd * DK:(hd + 1) * DK], ident)
                for hd in range(H):
                    x = pe.transpose(bk["kT"][0:DK, hd * P:(hd + 1) * P], qk[:, QW + hd * DK:QW + (hd + 1) * DK], ident)
                x.then_inc(qkT_ps, 1)

            def scores(n):
                pe.wait_ge(qT_rdy, n + 1)
                pe.wait_ge(kT_rdy, n + 1)
                for hd in range(H):
                    x = pe.matmul(bk["sc"][:, hd * P:(hd + 1) * P], qkT[:, H + hd, :], qkT[:, hd, :], start=True, stop=True)
                x.then_inc(sc_ps, 1)

            def outputs(n, j):
                pe.wait_ge(PT_rdy, n + 1)
                pe.wait_ge(Sm_rdy, 2 * n + 1)
                pe.wait_ge(v_rdy, n + 1)
                if late(n, 1):
                    pe.wait_ge(o_rdy, n)
                for hd in range(H):
                    out = bk["o"][:, hd * DV:(hd + 1) * DV]
                    pe.matmul(out, qkT[:, hd, :], Smid[:, hd, :], start=True, stop=False)
                    x = pe.matmul(out, PT[:, hd, :], v_sb[j][:, hd * DV:(hd + 1) * DV], start=False, stop=True)
                x.then_inc(o_ps, 1)
                for hd in range(H):
                    x = pe.matmul(bk["qT"][0:DK, hd * DV:(hd + 1) * DV], qk[:, QW + hd * DK:QW + (hd + 1) * DK],
                                  v_sb[j][:, hd * DV:(hd + 1) * DV], start=True, stop=True)
                x.then_inc(U_ps, 1)

            def gla(n, j):
                turn(n)
                z_lr(n + 1)
                z_qk(n + 1)
                lr_T(n + 1)
                scores(n)
                log_gate(n + 1)
                z_v(n + 1)
                cumulate(n + 1)
                outputs(n, j)
                z_og(n + 1)

            pe.wait_ge(cv_sb, 6 * CC)
            pe.wait_ge(wt_lo, 2 * KC)
            pe.wait_ge(c_in, 16 * (len(SMALL) + 1))
            z_lr(0)
            z_qk(0)
            lr_T(0)
            log_gate(0)
            z_v(0)
            cumulate(0)
            z_og(0)
            gla(0, 0)
            with pe.Fori(0, 3) as i:
                gla(2 * i + 1, 1)
                gla(2 * i + 2, 0)
            gla(NT - 2, 1)
            n = NT - 1
            turn(n)
            scores(n)
            def turn_o(n, j):
                pe.wait_ge(og_rdy, n + 1)
                if late(n, 1):
                    pe.wait_ge(catT_l, n)
                for hd in range(H):
                    x = pe.transpose(psum[:, 4, hd * P:(hd + 1) * P], og[j][:, hd * DV:(hd + 1) * DV], ident)
                x.then_inc(oT_ps, 1)

            pe.wait_ge(gog_rdy, NT)
            pe.wait_ge(v_rdy, NT)
            pe.wait_ge(E_rdy, NT)
            pe.wait_ge(conv, K * CC)
            pe.wait_ge(sconv, 2 * K)
            for part, src in enumerate([cT, csq]):
                for c in range(CC):
                    for b in range(NBLK):
                        if part and b == 0:
                            pe.wait_ge(csq_rdy, c + 1)
                        x = pe.matmul(psum[:, 3 * part + b, 0:BLK], C["ones"], src[:, c, b * BLK:(b + 1) * BLK],
                                      start=c == 0, stop=c == CC - 1)
            x.then_inc(st_ps, 1)
            pe.wait_ge(PT_rdy, n + 1)
            pe.wait_ge(o_rdy, n)
            pe.wait_ge(smp, 1)
            pe.wait_ge(s0_in, 16)
            for hd in range(H):
                out = bk["o"][0:NS, hd * DV:(hd + 1) * DV]
                for b in range(NB):
                    pe.matmul(out, qm[:, hd, b, :], s0[:, b, hd, :], start=b == 0, stop=False)
                x = pe.matmul(out, PT[:, hd, 0:NS], v_sb[0][:, hd * DV:(hd + 1) * DV], start=False, stop=True)
                if hd == 1:
                    pe.wait_ge(ln_v, 3)
                    turn_o(0, 0)
            x.then_inc(o_ps, 1)
            def project_part(j, half, chunks):
                for k in chunks:
                    for w, m in PASSES:
                        x = pe.matmul(psum[:, 2 * j + half, :], catT[j][w][:, k, :],
                                      wout[m][:, k, half * 512:(half + 1) * 512], start=k + w + m == 0,
                                      stop=k == KC - 1 and w == 1)
                return x

            def project(n, j, half):
                pe.wait_ge(catT_l, n + 1)
                pe.wait_ge(catT_c, 2 * n + 2)
                if late(n, 2):
                    pe.wait_ge(h_rdy, n - 1)
                early = isinstance(n, int) and n < 2
                project_part(j, half, range(H if early else 0, KC)).then_inc(w_ps, 1)

            pe.wait_ge(wl_lo, H)
            turn_o(1, 1)
            for n in range(2):
                pe.wait_ge(catT_l, n + 1)
                for half in range(2):
                    project_part(n, half, range(H))
            pe.wait_ge(o_rdy, NT)
            for b in range(NB):
                if b >= 3:
                    pe.wait_ge(SU_add, b - 2)
                for hd in range(H):
                    x = pe.matmul(psum[0:DK, 5 + b % 3, hd * DV:(hd + 1) * DV], km[:, b, hd * DK:(hd + 1) * DK],
                                  v_sb[0][:, hd * DV:(hd + 1) * DV], start=True, stop=True)
                x.then_inc(SU_ps, 1)

            def turn_xn2(n, j):
                pe.wait_ge(xn2_rdy, n + 1)
                for k in range(KC):
                    x = pe.transpose(psum[:, 5 + k // 4, (k % 4) * P:(k % 4 + 1) * P], xn2[j][:, k * P:(k + 1) * P], ident)
                x.then_inc(xn2T_ps, 1)

            def route(n, j):
                pe.wait_ge(xn2T_a, n + 1)
                pe.wait_ge(xn2T_v, n + 1)
                if late(n, 1):
                    pe.wait_ge(lg_rdy, n)
                for k in range(KC):
                    x = pe.matmul(psum[:, 7, 0:G + NE], xn2T[j][:, k, :], wr[:, k, :], start=k == 0, stop=k == KC - 1)
                x.then_inc(lg_ps, 1)

            def mix(n, j):
                project(n, j, 0)
                if late(n, 1):
                    turn_xn2(n - 1, 1 - j)
                if not (isinstance(n, int) and n in (0, NT - 1)):
                    turn_o(n + 1, 1 - j)
                project(n, j, 1)
                if late(n, 1):
                    route(n - 1, 1 - j)

            pe.wait_ge(SU_add, NB)
            pe.wait_ge(wl_lo, KC)
            tiles(pe, mix)
            turn_xn2(NT - 1, 0)
            route(NT - 1, 0)

            pe.wait_ge(M_rdy, 1)
            pe.matmul(psum[:, 0, 0:NT * NE], upper16[:], Msum, start=True, stop=True)
            pe.matmul(psum[:, 1, 0:NT * NE], ones16[:], Msum, start=True, stop=True).then_inc(rk_ps, 1)
            for m in range(2):
                pe.wait_ge(oh_rdy, m + 1)
                for n in range(m * NT, (m + 1) * NT):
                    x = pe.matmul(psum[:, 2, 0:NTILE], ohr[:, n, :], oht[:, n, :], start=n == 0, stop=n == 2 * NT - 1)
            x.then_inc(ids_ps, 1)

            def turn_rows(src, done):
                for k in range(KC):
                    x = pe.transpose(psum[:, k // 4, (k % 4) * P:(k % 4 + 1) * P], src[:, k * P:(k + 1) * P], ident)
                x.then_inc(done, 1)

            def turn_xg(t, sl, landed=None):
                pe.wait_ge(xg_in[sl], turn_of(t, sl) * 16 + 16 if landed is None else landed)
                turn_rows(xg[sl], xgT_ps)

            def mm_gate_up(sl, done):
                for k in range(KC):
                    x = pe.matmul(psum[:, 2 + sl, :], xgT[sl][:, k, :], wgu[sl][:, k, :], start=k == 0, stop=k == KC - 1)
                x.then_inc(done, 1)

            def mm_turn_h(done):
                for k in range(FC):
                    x = pe.transpose(psum[:, 5, k * P:(k + 1) * P], hg[:, k * P:(k + 1) * P], ident)
                x.then_inc(done, 1)

            def mm_down(sl, done):
                for half in range(2):
                    for k in range(FC):
                        x = pe.matmul(psum[:, 6 + half, :], hT[:, k, :], wdn[sl][:, k, half * 512:(half + 1) * 512],
                                      start=k == 0, stop=k == FC - 1)
                x.then_inc(done, 1)

            def down(t, sl, landed=None):
                pe.wait_ge(hT_rdy, t + 1)
                pe.wait_ge(dn_in[sl], turn_of(t, sl) * 16 + 16 if landed is None else landed)
                if late(t, 1):
                    pe.wait_ge(y_a, t)
                    pe.wait_ge(y_v, t)
                mm_down(sl, y_ps)

            def expert(t, sl):
                pe.wait_ge(xgT_a, t + 1)
                pe.wait_ge(xgT_v, t + 1)
                pe.wait_ge(gu_in[sl], turn_of(t, sl) * 16 + 16)
                mm_gate_up(sl, gu_ps)
                if isinstance(t, int) and t == NE - 1:
                    with pe.If(count > 0):
                        turn_xg(NE, 2, extra_turn(0, 2))
                else:
                    turn_xg(t + 1, (sl + 1) % 3)
                if late(t, 1):
                    down(t - 1, (sl - 1) % 3)
                pe.wait_ge(hg_rdy, t + 1)
                mm_turn_h(hT_ps)

            pe.wait_ge(pos_rdy, 1)
            count = pe.value_load(plan[0:1, EXTRA + 2:EXTRA + 3], min_val=0, max_val=EXTRA)
            turn_xg(0, 0)
            experts(pe, expert)
            with pe.If(count == 0):
                down(NE - 1, (NE - 1) % 3)

            def expert_extra(t, sl):
                pe.wait_ge(xgT_a, t + NE + 1)
                pe.wait_ge(xgT_v, t + NE + 1)
                pe.wait_ge(gu_in[sl], extra_turn(t, sl))
                mm_gate_up(sl, gu_ps)
                with pe.If(count > t + 1):
                    turn_xg(t + NE + 1, 3 - sl, extra_turn(t + 1, 3 - sl))
                down(t + NE - 1, 3 - sl, extra_turn(t - 1, 3 - sl))
                pe.wait_ge(hg_rdy, t + NE + 1)
                mm_turn_h(hT_ps)
                with pe.If(count == t + 1):
                    down(t + NE, sl, extra_turn(t, sl))

            extra(pe, count, expert_extra)
            pe.nop().then_inc(moe_done, 1)

            def turn_x3(n, j):
                pe.wait_ge(xn3_rdy, n + 1)
                if late(n, 1):
                    pe.wait_ge(x3T_v, n)
                turn_rows(xn3[j], x3T_ps)

            def project_p(n, j):
                if not late(n, 1):
                    pe.wait_ge(pw_in, 48)
                pe.wait_ge(pT_in[j], 8 * (n - j) + 16)
                if late(n, 1):
                    pe.wait_ge(mix_rdy, 2 * n - 1)
                for half in range(2):
                    for k in range(PC):
                        x = pe.matmul(psum[:, 4 + half, :], pT[j][:, k, :], wproj[:, k, half * 512:(half + 1) * 512],
                                      start=k == 0, stop=k == PC - 1)
                x.then_inc(pr_ps, 1)

            def gate_half(n, j, half):
                pe.wait_ge(x3T_v, n + 1)
                if late(n, 2):
                    pe.wait_ge(sg_rdy, n - 1)
                for k in range(KC):
                    for w, m in PASSES:
                        x = pe.matmul(psum[:, 2 + 4 * j + half, :], x3T[j][w][:, k, :],
                                      wgate[k][m][:, 0, half * 512:(half + 1) * 512], start=k + w + m == 0,
                                      stop=k == KC - 1 and w == 1)
                x.then_inc(gt_ps, 1)

            def embed(n, j):
                gate_half(n, j, 0)
                if late(n, 1):
                    project_p(n, j)
                if not (isinstance(n, int) and n == NT - 1):
                    turn_x3(n + 1, 1 - j)
                gate_half(n, j, 1)

            project_p(0, 0)
            turn_x3(0, 0)
            pe.wait_ge(wl_lo, 2 * KC)
            embeds(pe, embed)


def layout(x_prompt, x_sample, state_gla, state_conv, p_prompt, p_sample, g_mix, w_in, w_forget_up, b_forget, g_gla_out,
           w_conv, b_conv, g_conv_ln, b_conv_ln, w_out, g_ffn, w_grp_router, b_grp_router, w_exp_router, b_exp_router,
           w_exp_gate, w_exp_up, w_exp_down, g_ple, w_ple_gate, w_ple_proj, g_final):
    cat = np.concatenate

    def chunked(w):
        return np.swapaxes(w.reshape(-1, P, *w.shape[1:]), 0, 1)

    w = w_in[0]
    pad = NT * P - SEQ - NS
    w_cv = w[:, TW:].reshape(KC, P, 2, CC, P).transpose(3, 1, 0, 2, 4).reshape(CC, P, KC, 2 * P)
    return dict(
        consts=constants(),
        x=cat([x_prompt[0], x_sample.reshape(NS, D), np.zeros((pad, D), np.float32)]),
        w_tok=chunked(w[:, :TW]), w_cv=w_cv,
        state_conv=state_conv[0].transpose(2, 0, 1).reshape(CC, P, NB, HIST).transpose(1, 0, 2, 3),
        state_gla=state_gla[0].transpose(2, 0, 1, 3),
        w_conv=chunked(w_conv[0].T), conv_vecs=np.stack([v[0].reshape(CC, P).T for v in (b_conv, g_conv_ln, b_conv_ln)], 1),
        g_gla_out=g_gla_out[0][:, None], w_forget=cat([w_forget_up[0], b_forget]), w_out=chunked(w_out[0]),
        w_router=chunked(cat([w_grp_router[0], w_exp_router[0].transpose(1, 0, 2).reshape(D, NE)], 1)),
        b_router=cat([b_grp_router[0], b_exp_router[0].reshape(NE)])[None],
        w_gu=cat([w_exp_gate[0], w_exp_up[0]], -1).reshape(NE, KC, P, 2 * FF).transpose(0, 2, 1, 3),
        w_dn=w_exp_down[0].reshape(NE, FC, P, D).transpose(0, 2, 1, 3),
        w_ple=chunked(w_ple_gate[0]), w_proj=chunked(w_ple_proj[0]),
        pT=cat([p_prompt[0, 0], p_sample[0].reshape(NS, PLE), np.zeros((pad, PLE), np.float32)])
        .reshape(NT, P, PC, P).transpose(0, 3, 2, 1),
        g_mix=g_mix, g_ffn=g_ffn, g_ple=g_ple, g_final=g_final[None],
    )


OUTS = dict(y=(TOK, D), gla_prompt=(DK, H, DV), gla_sample=(DK, NB, H, DV), conv_prompt=(P, CC, HIST),
            conv_sample=(P, CC, NB, HIST))
SCRATCH = dict(xn2=((TOK, D), F32), yrows=((NTILE * P, D), F32))


def kernel(**inputs):
    import concourse.bacc as bacc
    from concourse.bass_utils import run_bass_kernel_spmd

    nc = bacc.Bacc("TRN2", target_bir_lowering=False, num_devices=1)
    arrays, ins, outs = {}, {}, {}
    for name, v in layout(**{k: np.asarray(x) for k, x in inputs.items()}).items():
        arrays["in_" + name] = v = np.ascontiguousarray(v)
        ins[name] = nc.dram_tensor("in_" + name, v.shape, mybir.dt.from_np(v.dtype), kind="ExternalInput").ap()
    for name, (shape, dt) in SCRATCH.items():
        ins[name] = nc.dram_tensor(name, shape, dt, kind="Internal").ap()
    for name, shape in OUTS.items():
        outs[name] = nc.dram_tensor("out_" + name, shape, F32, kind="ExternalOutput").ap()
    bass_decoder_step(nc, ins, outs)
    r = run_bass_kernel_spmd(nc, [arrays], core_ids=[0]).results[0]
    y = r["out_y"]
    return (y[None, :SEQ], y[SEQ:SEQ + NS].reshape(NB, TB, D),
            r["out_gla_prompt"].transpose(1, 0, 2)[None, None],
            r["out_gla_sample"].transpose(1, 2, 0, 3)[None],
            r["out_conv_prompt"].transpose(2, 1, 0).reshape(1, 1, HIST, CW),
            r["out_conv_sample"].transpose(2, 3, 1, 0).reshape(1, NB, HIST, CW))
```
